# Optimizing a Trainium2 kernel written in Bass

```python
import math, functools
import jax, jax.numpy as jnp
from jax import lax
import numpy as np

D_MODEL = 2048
BATCH = 1
SEQ = 512
DEPTH = 1
DEC_BATCH = 8
DEC_SEQ = 8
PAST_LEN = 4096
PAGE_SIZE = 128

D_PLE = 256
NORM_EPS = 1e-6
M_WIDTH = D_MODEL // 2
M_HEADS = 4
M_DH = M_WIDTH // M_HEADS
M_CONV = 4
M_CHUNK = 64
A_WIDTH = D_MODEL - M_WIDTH
A_HEADS = 16
A_DH = A_WIDTH // A_HEADS
A_KV = 4
A_GROUP = A_HEADS // A_KV
CMP_STRIDE = 16
CMP_LEN = 2 * CMP_STRIDE
CMP_HID = 64
SLC_BLK = 64
SLC_TOPN = 16
WINDOW = 512
Q_BLOCK = 128
KV_WIDTH = 6 * A_KV * A_DH
IN_SIZES = (M_WIDTH, M_WIDTH, M_WIDTH, M_HEADS, M_HEADS, A_WIDTH, KV_WIDTH, 3 * A_HEADS, A_WIDTH)
D_IN = sum(IN_SIZES)
SPLIT_AT = tuple(int(v) for v in np.cumsum(IN_SIZES)[:-1])

kernel_name = "hymba_mlstm_nsa_decoder_step"

def rms_norm(x, w):
    xf = x.astype(jnp.float32)
    y = xf * lax.rsqrt(jnp.mean(xf * xf, axis=-1, keepdims=True) + NORM_EPS)
    return (y * w.astype(jnp.float32)).astype(x.dtype)

def masked_softmax(s, mask):
    s = jnp.where(mask, s.astype(jnp.float32), -jnp.inf)
    m = jnp.max(s, axis=-1, keepdims=True)
    m = jnp.where(jnp.isfinite(m), m, 0.0)
    e = jnp.where(mask, jnp.exp(s - m), 0.0)
    return e / jnp.maximum(jnp.sum(e, axis=-1, keepdims=True), 1e-30)

def causal_conv(u, buf, w, b):
    T = u.shape[1]
    full = jnp.concatenate([buf.astype(u.dtype), u], axis=1)
    out = b + sum(full[:, j:j + T] * w[j] for j in range(M_CONV))
    return out, full[:, T:]

def mlstm_chunk(carry, inp):
    C, n, m = carry
    q, k, v, li, lf = inp
    L = q.shape[2]
    b = jnp.cumsum(lf, axis=-1)
    causal = jnp.tril(jnp.ones((L, L), dtype=bool))
    logd = jnp.where(causal, b[..., :, None] - b[..., None, :] + li[..., None, :], -jnp.inf)
    inter = b + m[..., None]
    m_t = jnp.maximum(inter, jnp.max(logd, axis=-1))
    s = jnp.einsum('bhtd,bhsd->bhts', q, k) * jnp.exp(logd - m_t[..., None])
    a = jnp.exp(inter - m_t)
    num = jnp.einsum('bhts,bhsv->bhtv', s, v) + a[..., None] * jnp.einsum('bhtd,bhdv->bhtv', q, C)
    den = jnp.sum(s, axis=-1) + a * jnp.einsum('bhtd,bhd->bht', q, n)
    h = num / jnp.maximum(jnp.abs(den), jnp.exp(-m_t))[..., None]
    b_end = b[..., -1]
    logw = b_end[..., None] - b + li
    m_new = jnp.maximum(b_end + m, jnp.max(logw, axis=-1))
    w = jnp.exp(logw - m_new[..., None])
    decay = jnp.exp(b_end + m - m_new)
    C_new = decay[..., None, None] * C + jnp.einsum('bhs,bhsd,bhsv->bhdv', w, k, v)
    n_new = decay[..., None] * n + jnp.einsum('bhs,bhsd->bhd', w, k)
    return (C_new, n_new, m_new), h

def mlstm_mixer(u, o_pre, z, i_pre, f_pre, conv_buf, C0, n0, m0,
                conv_w, conv_b, wq, wk, wv, b_i, b_f, norm_w):
    B, T, _ = u.shape
    c, new_buf = causal_conv(u, conv_buf, conv_w, conv_b)
    ch = jax.nn.silu(c).reshape(B, T, M_HEADS, M_DH)
    uh = u.reshape(B, T, M_HEADS, M_DH)
    q = jnp.einsum('bthc,hcd->bhtd', ch, wq).astype(jnp.float32)
    k = jnp.einsum('bthc,hcd->bhtd', ch, wk).astype(jnp.float32) * (M_DH ** -0.5)
    v = jnp.einsum('bthc,hcd->bhtd', uh, wv).astype(jnp.float32)
    li = (i_pre + b_i).astype(jnp.float32).transpose(0, 2, 1)
    lf = jax.nn.log_sigmoid((f_pre + b_f).astype(jnp.float32)).transpose(0, 2, 1)
    L = M_CHUNK if T % M_CHUNK == 0 else T
    nc = T // L

    def to_chunks(a):
        return jnp.moveaxis(a.reshape(a.shape[:2] + (nc, L) + a.shape[3:]), 2, 0)

    (C, n, m), h = lax.scan(mlstm_chunk,
                            (C0.astype(jnp.float32), n0.astype(jnp.float32), m0.astype(jnp.float32)),
                            (to_chunks(q), to_chunks(k), to_chunks(v), to_chunks(li), to_chunks(lf)))
    h = jnp.moveaxis(h, 0, 2).reshape(B, M_HEADS, T, M_DH).transpose(0, 2, 1, 3)
    h = h * jax.nn.sigmoid(o_pre.astype(jnp.float32)).reshape(B, T, M_HEADS, M_DH)
    h = rms_norm(h, norm_w).reshape(B, T, M_WIDTH)
    out = (h * jax.nn.silu(z.astype(jnp.float32))).astype(u.dtype)
    return out, new_buf, C, n, m

def compress(rows, pe, w1, w2, k_norm):
    B, L = rows.shape[:2]
    n_seg = L // CMP_STRIDE
    seg = rows[:, :n_seg * CMP_STRIDE].reshape(B, n_seg, CMP_STRIDE, 2, A_KV, A_DH)
    w1r = w1.reshape(2, 2, CMP_STRIDE, A_DH, CMP_HID)
    per = jnp.einsum('bnjcgd,cxjdh->bnxcgh', seg, w1r)
    bias = jnp.einsum('cxjd,cxjdh->ch', pe.reshape(2, 2, CMP_STRIDE, A_DH), w1r)
    hid = per[:, :-1, 0] + per[:, 1:, 1] + bias[:, None, :]
    out = jnp.einsum('bncgh,chd->bncgd', jax.nn.silu(hid), w2)
    return rms_norm(out[:, :, 0], k_norm), out[:, :, 1]

def cmp_end_positions(n_cmp):
    return jnp.arange(n_cmp, dtype=jnp.int32) * CMP_STRIDE + (CMP_LEN - 1)

def nsa_compressed(q, tq, kc, vc, c_end, n_slc):
    Tq = q.shape[0]
    qg = q.reshape(Tq, A_KV, A_GROUP, A_DH)
    s = jnp.einsum('tgad,ngd->tgan', qg, kc) * (A_DH ** -0.5)
    p = masked_softmax(s, (c_end[None, :] <= tq[:, None])[:, None, None, :])
    o = jnp.einsum('tgan,ngd->tgad', p, vc)
    pg = jnp.sum(p, axis=2)
    n_cmp = kc.shape[0]
    r = SLC_BLK // CMP_STRIDE
    pad_back = r * (n_slc + 1) - 1 - n_cmp
    pp = jnp.pad(pg, ((0, 0), (0, 0), (1, pad_back))).reshape(Tq, A_KV, n_slc + 1, r)
    ps = jnp.sum(pp[..., :-1, :], axis=-1) + pp[..., 1:, 0]
    blk = jnp.arange(n_slc, dtype=jnp.int32)[None, :]
    valid = blk * SLC_BLK <= tq[:, None]
    cur = (tq // SLC_BLK)[:, None]
    forced = (blk == 0) | (blk == cur) | (blk == cur - 1)
    score = jnp.where(valid[:, None], jnp.where(forced[:, None], jnp.inf, ps), -jnp.inf)
    _, idx = lax.top_k(score, min(SLC_TOPN, n_slc))
    return o, idx

def nsa_combine(q, tq, o_cmp, idx, k_sel, v_sel, kw, vw, pw, g):
    Tq = q.shape[0]
    qg = q.reshape(Tq, A_KV, A_GROUP, A_DH)
    scale = A_DH ** -0.5
    pos = idx[..., None] * SLC_BLK + jnp.arange(SLC_BLK, dtype=jnp.int32)
    s = jnp.einsum('tgad,tgmd->tgam', qg, k_sel.reshape(Tq, A_KV, -1, A_DH)) * scale
    p = masked_softmax(s, (pos <= tq[:, None, None, None]).reshape(Tq, A_KV, 1, -1))
    o_sel = jnp.einsum('tgam,tgmd->tgad', p, v_sel.reshape(Tq, A_KV, -1, A_DH))
    diff = tq[:, None] - pw[None, :]
    wmask = (pw[None, :] >= 0) & (diff >= 0) & (diff < WINDOW)
    s = jnp.einsum('tgad,sgd->tgas', qg, kw) * scale
    p = masked_softmax(s, wmask[:, None, None, :])
    o_win = jnp.einsum('tgas,sgd->tgad', p, vw)
    gg = g.astype(jnp.float32).reshape(Tq, 3, A_KV, A_GROUP)[..., None]
    o = gg[:, 0] * o_cmp + gg[:, 1] * o_sel + gg[:, 2] * o_win
    return o.reshape(Tq, A_WIDTH)

def nsa_prompt(q, g, kv, cmp_pe, cmp_w1, cmp_w2, k_norm_cmp):
    B, T = q.shape[:2]
    kc, vc = compress(kv[:, :, 0:2], cmp_pe, cmp_w1, cmp_w2, k_norm_cmp)
    c_end = cmp_end_positions(kc.shape[1])
    n_slc = T // SLC_BLK
    k_blk = kv[:, :, 2].reshape(B, n_slc, SLC_BLK, A_KV, A_DH).transpose(0, 3, 1, 2, 4)
    v_blk = kv[:, :, 3].reshape(B, n_slc, SLC_BLK, A_KV, A_DH).transpose(0, 3, 1, 2, 4)
    win = jnp.pad(kv[:, :, 4:6], ((0, 0), (WINDOW, 0), (0, 0), (0, 0), (0, 0)))
    nqb = T // Q_BLOCK
    qr = q.astype(jnp.float32).reshape(B, nqb, Q_BLOCK, A_HEADS, A_DH)
    gr = g.reshape(B, nqb, Q_BLOCK, 3, A_HEADS)
    g_ax = jnp.arange(A_KV)[None, :, None]

    def one(ids):
        b, qb = ids[0], ids[1]
        t0 = qb * Q_BLOCK
        tq = t0 + jnp.arange(Q_BLOCK, dtype=jnp.int32)
        qq = qr[b, qb]
        o_cmp, idx = nsa_compressed(qq, tq, kc[b], vc[b], c_end, n_slc)
        k_sel = k_blk[b][g_ax, idx]
        v_sel = v_blk[b][g_ax, idx]
        w = lax.dynamic_slice_in_dim(win[b], t0, Q_BLOCK + WINDOW, axis=0)
        pw = t0 - WINDOW + jnp.arange(Q_BLOCK + WINDOW, dtype=jnp.int32)
        return nsa_combine(qq, tq, o_cmp, idx, k_sel, v_sel, w[:, 0], w[:, 1], pw, gr[b, qb])

    ids = jnp.stack([jnp.repeat(jnp.arange(B, dtype=jnp.int32), nqb),
                     jnp.tile(jnp.arange(nqb, dtype=jnp.int32), B)], axis=-1)
    return lax.map(one, ids).reshape(B, T, A_WIDTH)

def nsa_sample(q, g, kv, cache_kv, win_buf, page_table, layer, cmp_pe, cmp_w1, cmp_w2, k_norm_cmp):
    Bd, Ts = q.shape[:2]
    n_pages = page_table.shape[1]
    past_len = n_pages * PAGE_SIZE
    past = cache_kv[layer, page_table, :, 0:2].reshape(Bd, past_len, 2, A_KV, A_DH).astype(kv.dtype)
    kc, vc = compress(jnp.concatenate([past, kv[:, :, 0:2]], axis=1), cmp_pe, cmp_w1, cmp_w2, k_norm_cmp)
    c_end = cmp_end_positions(kc.shape[1])
    n_past_blk = past_len // SLC_BLK
    n_new_blk = -(-Ts // SLC_BLK)
    n_slc = n_past_blk + n_new_blk
    blk_per_page = PAGE_SIZE // SLC_BLK
    new_blk = jnp.pad(kv[:, :, 2:4], ((0, 0), (0, n_new_blk * SLC_BLK - Ts), (0, 0), (0, 0), (0, 0)))
    new_blk = new_blk.reshape(Bd, n_new_blk, SLC_BLK, 2, A_KV, A_DH)
    wb = win_buf.shape[1]
    tq = past_len + jnp.arange(Ts, dtype=jnp.int32)
    pw = past_len - wb + jnp.arange(wb + Ts, dtype=jnp.int32)
    g_ax = jnp.arange(A_KV)[None, :, None, None]
    r_blk = jnp.arange(SLC_BLK, dtype=jnp.int32)

    def one(qq, gg, kc_b, vc_b, new_b, kvw_b, win_b, pt_row):
        o_cmp, idx = nsa_compressed(qq, tq, kc_b, vc_b, c_end, n_slc)
        pidx = jnp.minimum(idx, n_past_blk - 1)
        page = pt_row[pidx // blk_per_page][..., None]
        rows = ((pidx % blk_per_page) * SLC_BLK)[..., None] + r_blk
        nidx = jnp.clip(idx - n_past_blk, 0, n_new_blk - 1)[..., None]
        is_new = (idx >= n_past_blk)[..., None, None]
        k_sel = jnp.where(is_new, new_b[nidx, r_blk, 0, g_ax], cache_kv[layer, page, rows, 2, g_ax])
        v_sel = jnp.where(is_new, new_b[nidx, r_blk, 1, g_ax], cache_kv[layer, page, rows, 3, g_ax])
        kw = jnp.concatenate([win_b[:, 0].astype(kvw_b.dtype), kvw_b[:, 0]], axis=0)
        vw = jnp.concatenate([win_b[:, 1].astype(kvw_b.dtype), kvw_b[:, 1]], axis=0)
        return nsa_combine(qq, tq, o_cmp, idx, k_sel, v_sel, kw, vw, pw, gg)

    return jax.vmap(one)(q.astype(jnp.float32), g, kc, vc, new_blk, kv[:, :, 4:6], win_buf, page_table)

def mixer_inputs(x, norm_w, w_in, a_q_norm, a_k_norm):
    B, T, _ = x.shape
    xn = rms_norm(x, norm_w)
    u, o, mz, ig, fg, q, kv, g, az = jnp.split(xn @ w_in, SPLIT_AT, axis=-1)
    q = rms_norm(q.reshape(B, T, A_HEADS, A_DH), a_q_norm)
    kv = kv.reshape(B, T, 6, A_KV, A_DH)
    kv = jnp.stack([kv[:, :, 0], kv[:, :, 1], rms_norm(kv[:, :, 2], a_k_norm[1]), kv[:, :, 3],
                    rms_norm(kv[:, :, 4], a_k_norm[2]), kv[:, :, 5]], axis=2)
    g = jax.nn.sigmoid(g).reshape(B, T, 3, A_HEADS)
    return (u, o, mz, ig, fg), (q, kv, g, az)

def mixer_output(x, m_out, a_out, p, w_out, ple_proj, ple_norm, ple_gate):
    h = x + jnp.concatenate([m_out, a_out.astype(x.dtype)], axis=-1) @ w_out
    gate = jax.nn.sigmoid(rms_norm(h, ple_norm) @ ple_gate)
    return h + gate * (p @ ple_proj)

def setup_inputs(seed: int = 0) -> dict:
    key = jax.random.key(seed)
    ks = iter(jax.random.split(key, 40))
    f32 = jnp.float32

    def nrm(shape, scale):
        return jax.random.normal(next(ks), shape, f32) * scale

    n_pages = PAST_LEN // PAGE_SIZE
    n_used = DEC_BATCH * n_pages
    n_pool = n_used + (n_used + 3) // 4
    wb = min(WINDOW, PAST_LEN)
    page_table = jax.random.permutation(next(ks), n_pool)[:n_used].reshape(DEC_BATCH, n_pages).astype(jnp.int32)
    return {
        "x_prompt": nrm((BATCH, SEQ, D_MODEL), 1.0),
        "x_sample": nrm((DEC_BATCH, DEC_SEQ, D_MODEL), 1.0),
        "cache_nsa_kv": nrm((DEPTH, n_pool, PAGE_SIZE, 4, A_KV, A_DH), 1.0),
        "cache_win_kv": nrm((DEPTH, DEC_BATCH, wb, 2, A_KV, A_DH), 1.0),
        "state_mlstm_C": nrm((DEPTH, DEC_BATCH, M_HEADS, M_DH, M_DH), 1.0),
        "state_mlstm_n": nrm((DEPTH, DEC_BATCH, M_HEADS, M_DH), 1.0),
        "state_mlstm_m": nrm((DEPTH, DEC_BATCH, M_HEADS), 1.0),
        "state_mlstm_conv": nrm((DEPTH, DEC_BATCH, M_CONV - 1, M_WIDTH), 1.0),
        "page_table": page_table,
        "p_prompt": nrm((DEPTH, BATCH, SEQ, D_PLE), 1.0),
        "p_sample": nrm((DEPTH, DEC_BATCH, DEC_SEQ, D_PLE), 1.0),
        "norm_w": 1.0 + nrm((DEPTH, D_MODEL), 0.02),
        "w_in": nrm((DEPTH, D_MODEL, D_IN), D_MODEL ** -0.5),
        "m_conv_w": nrm((DEPTH, M_CONV, M_WIDTH), M_CONV ** -0.5),
        "m_conv_b": nrm((DEPTH, M_WIDTH), 0.02),
        "m_wq": nrm((DEPTH, M_HEADS, M_DH, M_DH), M_DH ** -0.5),
        "m_wk": nrm((DEPTH, M_HEADS, M_DH, M_DH), M_DH ** -0.5),
        "m_wv": nrm((DEPTH, M_HEADS, M_DH, M_DH), M_DH ** -0.5),
        "m_b_i": nrm((DEPTH, M_HEADS), 0.1),
        "m_b_f": jnp.linspace(3.0, 6.0, M_HEADS, dtype=f32)[None, :] + nrm((DEPTH, M_HEADS), 0.1),
        "m_norm_w": 1.0 + nrm((DEPTH, M_HEADS, M_DH), 0.02),
        "a_q_norm": 1.0 + nrm((DEPTH, A_DH), 0.02),
        "a_k_norm": 1.0 + nrm((DEPTH, 3, A_DH), 0.02),
        "cmp_pe": nrm((DEPTH, 2, CMP_LEN, A_DH), 0.02),
        "cmp_w1": nrm((DEPTH, 2, CMP_LEN, A_DH, CMP_HID), (CMP_LEN * A_DH) ** -0.5),
        "cmp_w2": nrm((DEPTH, 2, CMP_HID, A_DH), CMP_HID ** -0.5),
        "w_out": nrm((DEPTH, M_WIDTH + A_WIDTH, D_MODEL), (M_WIDTH + A_WIDTH) ** -0.5),
        "ple_proj": nrm((DEPTH, D_PLE, D_MODEL), D_PLE ** -0.5),
        "ple_norm": 1.0 + nrm((DEPTH, D_MODEL), 0.02),
        "ple_gate": nrm((DEPTH, D_MODEL, D_MODEL), D_MODEL ** -0.5),
    }

def reference(x_prompt, x_sample, cache_nsa_kv, cache_win_kv, state_mlstm_C, state_mlstm_n,
              state_mlstm_m, state_mlstm_conv, page_table, p_prompt, p_sample, norm_w, w_in,
              m_conv_w, m_conv_b, m_wq, m_wk, m_wv, m_b_i, m_b_f, m_norm_w, a_q_norm, a_k_norm,
              cmp_pe, cmp_w1, cmp_w2, w_out, ple_proj, ple_norm, ple_gate):
    xp, xs = x_prompt, x_sample
    B, T = xp.shape[:2]
    per_layer = []
    for i in range(DEPTH):
        mw = (m_conv_w[i], m_conv_b[i], m_wq[i], m_wk[i], m_wv[i], m_b_i[i], m_b_f[i], m_norm_w[i])
        cw = (cmp_pe[i], cmp_w1[i], cmp_w2[i], a_k_norm[i, 0])
        ow = (w_out[i], ple_proj[i], ple_norm[i], ple_gate[i])
        (u, o, mz, ig, fg), (q, kv, g, az) = mixer_inputs(xp, norm_w[i], w_in[i], a_q_norm[i], a_k_norm[i])
        m_out, conv_p, C_p, n_p, m_p = mlstm_mixer(
            u, o, mz, ig, fg, jnp.zeros((B, M_CONV - 1, M_WIDTH), u.dtype),
            jnp.zeros((B, M_HEADS, M_DH, M_DH), jnp.float32), jnp.zeros((B, M_HEADS, M_DH), jnp.float32),
            jnp.full((B, M_HEADS), -jnp.inf, jnp.float32), *mw)
        a_out = nsa_prompt(q, g, kv, *cw) * jax.nn.silu(az.astype(jnp.float32))
        xp_new = mixer_output(xp, m_out, a_out, p_prompt[i], *ow)
        kv_p = kv[:, :, 0:4]
        win_p = kv[:, -min(WINDOW, T):, 4:6]
        (u, o, mz, ig, fg), (q, kv, g, az) = mixer_inputs(xs, norm_w[i], w_in[i], a_q_norm[i], a_k_norm[i])
        m_out, conv_s, C_s, n_s, m_s = mlstm_mixer(
            u, o, mz, ig, fg, state_mlstm_conv[i], state_mlstm_C[i], state_mlstm_n[i], state_mlstm_m[i], *mw)
        a_out = nsa_sample(q, g, kv, cache_nsa_kv, cache_win_kv[i], page_table, i, *cw)
        a_out = a_out * jax.nn.silu(az.astype(jnp.float32))
        xs_new = mixer_output(xs, m_out, a_out, p_sample[i], *ow)
        kv_s = kv[:, :, 0:4]
        wb = cache_win_kv.shape[2]
        win_s = jnp.concatenate([cache_win_kv[i].astype(kv.dtype), kv[:, :, 4:6]], axis=1)[:, -wb:]
        per_layer.append((kv_p, kv_s, win_p, win_s, C_p, n_p, m_p, conv_p, C_s, n_s, m_s, conv_s))
        xp, xs = xp_new, xs_new
    (kv_p, kv_s, win_p, win_s, C_p, n_p, m_p, conv_p,
     C_s, n_s, m_s, conv_s) = [jnp.stack(a, axis=0) for a in zip(*per_layer)]
    return (xp, xs, kv_p, kv_s, win_p, win_s, C_p, n_p, m_p, conv_p, C_s, n_s, m_s, conv_s)


_drawn_inputs = setup_inputs


def setup_inputs(seed=0):
    import zlib

    import numpy as np

    out = dict(_drawn_inputs(seed))
    spreads = {}
    factors = {'cache_nsa_kv': 4.017,
     'm_norm_w': 8.0,
     'a_q_norm': 8.0,
     'a_k_norm': 4.177,
     'cmp_pe': 8.0,
     'ple_norm': 8.0}
    for name, (base, spread) in spreads.items():
        noise = np.random.default_rng([zlib.crc32(name.encode()), seed]).standard_normal(out[name].shape)
        drawn = base * np.exp(spread * noise) if base else spread * noise
        out[name] = __import__('jax').numpy.asarray(drawn.astype(out[name].dtype))
    for name, factor in factors.items():
        out[name] = (out[name] * factor).astype(out[name].dtype)
    return out
```

```python
from contextlib import ExitStack

import numpy as np

import concourse.bass as bass
from concourse import mybir

F32 = mybir.dt.float32
F32R = mybir.dt.float32r
I32 = mybir.dt.int32
ALU = mybir.AluOpType
ACT = mybir.ActivationFunctionType
AX = mybir.AxisListType.X

P = 128
D = 2048
KD = D // P
TP = 512
NB = 8
TS = 8
TSA = NB * TS
T = TP + TSA
TILES = [(t, min(P, T - t)) for t in range(0, T, P)]
D_PLE = 256
PAST = 4096
PAGE = 128
NPG = PAST // PAGE
EPS = 1e-6
MH, MD, MW = 4, 256, 1024
CONV = 4
AH, AD, KV = 16, 64, 4
GRP = AH // KV
AW = 1024
SEG, CLEN = 16, 32
BLK, TOPN = 64, 16
WIN = 512
CH = 512
NEG = -1e30
SCALE = float(AD) ** -0.5
PADW = TP + CONV - 1
SPAD = TS + CONV - 1
NCMP_P = TP // SEG - 1
NCMP_S = PAST // SEG - 1
NBLK = PAST // BLK + 1

C_U, C_O, C_Z, C_IF, C_Q = 0, MW, 2 * MW, 3 * MW, 3 * MW + 2 * MH
C_KV = C_Q + AW
C_G = C_KV + 6 * KV * AD
C_AZ = C_G + 3 * AH
NGATE = 2 * MH + 3 * AH


class Chain:

    def __init__(self, eng, sem, base=0):
        self.eng, self.sem, self.base, self.n = eng, sem, base, 0

    def __call__(self, ins):
        self.n += 1
        ins.then_inc(self.sem, 1)
        self.eng.wait_ge(self.sem, self.base + self.n)


class Semaphores:

    def __init__(self, nc):
        self.nc, self.stack, self.nums = nc, ExitStack(), []

    def __enter__(self):
        return self

    def __call__(self, name):
        handle = self.stack.enter_context(self.nc.semaphore(name))
        self.nums.append(handle.num)
        return handle

    def __exit__(self, *failed):
        if not any(failed):
            nums = sorted(self.nums)
            starts = [n for n in nums if n - 1 not in nums]
            for start in starts:
                end = next(n for n in range(start, max(nums) + 2) if n not in nums)
                self.nc.all_engine_barrier(sems_to_clear=range(start, end))
        self.stack.close()


class Buffers:
    pass


def constants(nc, B, a):
    with Semaphores(nc) as sem, ExitStack() as ctx:
        pool_step, vec_step, iotas, small_loads = sem("pool_step"), sem("vec_step"), sem("iotas"), sem("small_loads")
        scratch = lambda n, s, d: ctx.enter_context(nc.sbuf_tensor(n, s, d))
        row = scratch("c_row", [P, 1], I32)
        row_t = scratch("c_row_t", [P, 1], I32)
        row_gt = scratch("c_row_gt", [P, 1], I32)
        row_tf = scratch("c_row_tf", [P, 1], F32)
        row_gtf = scratch("c_row_gtf", [P, 1], F32)
        col32 = scratch("c_col32", [P, 32], F32)
        col128 = scratch("c_col128", [32, P], I32)
        col128b = scratch("c_col128b", [32, P], I32)
        col128f = scratch("c_col128f", [32, P], F32)
        part = scratch("c_part", [32, 1], F32)
        block = ctx.enter_context(nc.Block())

        SMALL = 11

        @block.sync
        def _(sp):
            small = [
                (B.normw, a["norm_w"]), (B.plenw, a["ple_norm"]), (B.convw, a["conv_w"]), (B.convb, a["conv_b"]),
                (B.qnw[0:64, :], a["a_q_norm"].rearrange("(d x) -> d x", x=1)),
                (B.qnw[64:128, :], a["a_q_norm"].rearrange("(d x) -> d x", x=1)),
                (B.knw, a["a_k_norm"].rearrange("a d -> (a d)").partition_broadcast(P)),
                (B.cw2, a["cmp_w2"]),
                (B.bif, a["b_if"]), (B.m0, a["m0"]), (B.ptab, a["page_table"]),
            ]
            assert len(small) == SMALL
            for dst, src in small:
                sp.dma_start(dst if isinstance(dst, bass.AP) else dst[:], src).then_inc(small_loads, 16)
            sp.wait_ge(small_loads, 16 * len(small))

        @block.gpsimd
        def _(pool):
            step = Chain(pool, pool_step)
            g = nc.gpsimd
            step(g.memset(B.ident[:], 0.0))
            step(g.affine_select(out=B.ident[:], in_=B.ident[:], compare_op=ALU.not_equal, fill=1.0, base=0,
                                 pattern=[[-1, P]], channel_multiplier=1))
            step(g.memset(B.causal[:], 0.0))
            step(g.affine_select(out=B.causal[:], in_=B.causal[:], compare_op=ALU.is_ge, fill=NEG, base=0,
                                 pattern=[[-1, P]], channel_multiplier=1))
            step(g.memset(B.cmpmask[:], 0.0))
            step(g.affine_select(out=B.cmpmask[:], in_=B.cmpmask[:], compare_op=ALU.is_ge, fill=NEG, base=-(CLEN - 1),
                                 pattern=[[P, 4], [-SEG, 32]], channel_multiplier=1))
            step(g.memset(B.blockdiag[:], 1.0))
            step(g.affine_select(out=B.blockdiag[:], in_=B.blockdiag[:], compare_op=ALU.is_ge, fill=0.0, base=0,
                                 pattern=[[TS, NB], [1, TS]], channel_multiplier=-1))
            step(g.affine_select(out=B.blockdiag[:], in_=B.blockdiag[:], compare_op=ALU.is_ge, fill=0.0, base=0,
                                 pattern=[[-TS, NB], [0, TS]], channel_multiplier=1))
            step(g.memset(B.member[:], 1.0))
            step(g.affine_select(out=B.member[:], in_=B.member[:], compare_op=ALU.is_ge, fill=0.0, base=0,
                                 pattern=[[-TS, NB]], channel_multiplier=1))
            step(g.affine_select(out=B.member[:], in_=B.member[:], compare_op=ALU.is_ge, fill=0.0, base=TS - 1,
                                 pattern=[[TS, NB]], channel_multiplier=-1))
            step(g.memset(B.headsel[:], 0.0))
            step(g.affine_select(out=B.headsel[:], in_=B.headsel[:], compare_op=ALU.not_equal, fill=1.0, base=0,
                                 pattern=[[-1, MH], [0, P]], channel_multiplier=1))
            step(g.iota(row[:], pattern=[[0, 1]], base=0, channel_multiplier=1))
            step(g.iota(col32[:], pattern=[[1, 32]], base=0, channel_multiplier=0, allow_small_or_imprecise_dtypes=True))
            step(g.iota(col128[:], pattern=[[1, P]], base=0, channel_multiplier=0))
            g.iota(part[:], pattern=[[0, 1]], base=0, channel_multiplier=1,
                   allow_small_or_imprecise_dtypes=True).then_inc(iotas, 1)

        @block.vector
        def _(dve):
            step = Chain(dve, vec_step)
            v = nc.vector
            v.memset(B.ones[:], 1.0)
            step(v.memset(B.eps[:], EPS))
            step(v.memset(B.keep[:], 1.0))
            step(v.memset(B.keep[:, TP:T].rearrange("p (b t) -> p b t", t=TS)[:, :, 0:1], 0.0))
            step(v.memset(B.restart[:], 0.0))
            step(v.memset(B.restart[:, TP:T].rearrange("p (b t) -> p b t", t=TS)[:, :, 0:1], NEG))
            step(v.memset(B.newmask[:], NEG))
            dve.wait_ge(small_loads, 16 * SMALL)
            step(v.tensor_scalar(B.qnw[:], B.qnw[:], SCALE, None, ALU.mult))
            dve.wait_ge(iotas, 1)
            step(v.tensor_scalar(row_t[:], row[:], TS - 1, None, ALU.bitwise_and))
            step(v.tensor_scalar(row_gt[:], row[:], 5, 3, ALU.logical_shift_right, ALU.logical_shift_left))
            step(v.tensor_tensor(row_gt[:], row_gt[:], row_t[:], ALU.bitwise_or))
            step(v.tensor_copy(row_tf[:], row_t[:]))
            step(v.tensor_copy(row_gtf[:], row_gt[:]))
            step(v.tensor_scalar(B.fold[:], col32[:], row_gtf[:, 0:1], None, ALU.is_equal))
            step(v.tensor_scalar(col128b[:], col128[:], TS - 1, None, ALU.bitwise_and))
            step(v.tensor_scalar(col128[:], col128[:], 5, 3, ALU.logical_shift_right, ALU.logical_shift_left))
            step(v.tensor_tensor(col128[:], col128[:], col128b[:], ALU.bitwise_or))
            step(v.tensor_copy(col128f[:], col128[:]))
            step(v.tensor_scalar(B.unfold[:], col128f[:], part[:, 0:1], None, ALU.is_equal))
            step(v.tensor_scalar(B.newmask[:].rearrange("p (b x) -> p b x", x=TSA + TS)[:, :, 0:TS],
                                 col32[:, 0:TS].unsqueeze(1).to_broadcast([P, NB, TS]), row_tf[:, 0:1], NEG,
                                 ALU.is_gt, ALU.mult))
            step(v.tensor_scalar(B.winmask[:], col32[:, 0:TS], row_tf[:, 0:1], NEG, ALU.is_le, ALU.mult))


def plan_projection():
    chunks = [("kv", 0), ("kv", 1), ("kv", 2), ("q", 0), ("q", 1), ("if", 0), ("u", 0), ("u", 1),
              ("o", 0), ("o", 1), ("z", 0), ("z", 1), ("az", 0), ("az", 1)]
    units = []
    for c, (kind, n) in enumerate(chunks):
        if kind == "u":
            for m in range(4):
                units += [(c, kind, n, m, 0), (c, kind, n, m, 1)]
        else:
            units += [(c, kind, n, t, 0) for t in range(len(TILES))]
    return chunks, units


def project_in(nc, B, a, o):
    chunks, units = plan_projection()
    NM, NSTG = 4, 3
    staged = ("kv", "q", "o", "z", "az")
    slot, trans, outdma = {}, {}, {}
    n = 0
    for u, (c, kind, ch, t, h) in enumerate(units):
        if kind in staged:
            slot[u] = n
            n += 1
        prompt = t < 4
        if (kind == "kv" and (ch == 1 or ch == 2 or prompt)) or kind == "q":
            trans[u] = len(trans)
        if kind in ("kv", "o", "z", "az"):
            outdma[u] = len(outdma)
    user = {k: u for u, k in slot.items()}
    vec_count = {}
    for u in slot:
        if units[u][1:3] != ("kv", 0):
            vec_count[u] = len(vec_count) + 1
    last_unit = {}
    for u, (c, *_rest) in enumerate(units):
        last_unit[c] = u
    with Semaphores(nc) as sem, ExitStack() as ctx:
        sb = lambda n, s, d=F32: ctx.enter_context(nc.sbuf_tensor(n, s, d))
        ps = lambda n, s: ctx.enter_context(nc.psum_tensor(n, s, F32))
        sq = sb("xsq", [P, 2, T])
        rstd = sb("x_rstd", [P, T])
        stg = sb("stg", [P, NSTG, CH])
        stg2, msq = sq[:, 0, 0:CH], sq[:, 1, 0:CH]
        ms = sb("ms", [P, 8])
        dup = sb("dup", [P, KV, 2, AD])
        mm = ps("mm", [P, NM, CH])
        tr = ps("tr", [P, 2, CH])
        ssq = ps("ssq", [P, CH])
        ssq2 = ps("ssq2", [P, TSA])
        x_in, squared, summed, rs_ready = sem("x_in"), sem("squared"), sem("summed"), sem("rs_ready")
        normed = sem("normed")
        w_in_sem = [sem("w_in0"), sem("w_in1")]
        mm_done, evac = sem("mm_done"), sem("evac")
        ms_ready, rstd_ready = sem("ms_ready"), sem("rstd_ready")
        unit_ready = sem("unit_ready")
        tr_done, tr_evac = sem("tr_done"), sem("tr_evac")
        out_sem = [sem(f"out_stage{i}") for i in range(NSTG)]
        act_step, dve_step = sem("p_act_step"), sem("p_dve_step")

        def ready(u):
            return (unit_ready, vec_count[u]) if u in vec_count else (evac, u + 1)

        def dup_free(u):
            users = [w for w in range(u) if w in trans and ((units[w][1] == "kv" and units[w][2] > 0 and units[w][3] < 4)
                                                            or (units[w][1] == "q" and units[w][3] == 4))]
            return trans[users[-1]] + 1 if users else 0

        block = ctx.enter_context(nc.Block())
        w_view = a["w_in"].rearrange("(k p) n -> p k n", p=P)
        col0 = {"u": C_U, "o": C_O, "z": C_Z, "q": C_Q, "kv": C_KV, "az": C_AZ}

        @block.sync
        def _(sp):
            def load(c):
                kind, ch = chunks[c]
                if c >= 2:
                    sp.wait_ge(mm_done, last_unit[c - 2] + 1)
                if kind == "if":
                    sp.dma_start(B.wb[:, c % 2, :, 0:2 * MH], w_view[:, :, C_IF:C_IF + 2 * MH]).then_inc(w_in_sem[c % 2], 16)
                    sp.dma_start(B.wb[:, c % 2, :, 2 * MH:NGATE], w_view[:, :, C_G:C_G + 3 * AH]).then_inc(w_in_sem[c % 2], 16)
                else:
                    for half in range(2):
                        ks = slice(half * 8, half * 8 + 8)
                        c0 = col0[kind] + ch * CH
                        sp.dma_start(B.wb[:, c % 2, ks, :], w_view[:, ks, c0:c0 + CH]).then_inc(w_in_sem[c % 2], 16)

            def store(u):
                c, kind, ch, t, h = units[u]
                t0, n = TILES[t]
                s = slot[u] % NSTG
                sp.wait_ge(*ready(u))
                if kind == "kv" and ch < 2:
                    dst = (o["kv_prompt"][t0:t0 + n, ch * CH:(ch + 1) * CH] if t < 4
                           else o["kv_sample"][:, ch * CH:(ch + 1) * CH])
                elif kind == "kv":
                    dst = o["win_prompt"][t0:t0 + n, :] if t < 4 else o["win_sample"][:, WIN - TS:WIN, :]
                else:
                    which = {"o": 0, "z": 1, "az": 2}[kind]
                    dst = B.gates_dram[which, t0:t0 + n, ch * CH:(ch + 1) * CH]
                sp.dma_start(dst, stg[0:n, s, :]).then_inc(out_sem[s], 16)

            sp.dma_start(B.feat[:], a["x_fm"]).then_inc(x_in, 16)
            load(0)
            load(1)
            for u, unit in enumerate(units):
                c = unit[0]
                if u == last_unit[c] and c + 2 < len(chunks):
                    load(c + 2)
                if u in outdma:
                    store(u)
            for s in range(NSTG):
                sp.wait_ge(out_sem[s], 16 * sum(1 for u in outdma if slot[u] % NSTG == s))

        @block.tensor
        def _(pe):
            for k in range(KD):
                pe.wait_ge(squared, k + 1)
                nc.tensor.matmul(ssq[:], B.ones[:], sq[:, k % 2, 0:TP], start=k == 0, stop=k == KD - 1)
                nc.tensor.matmul(ssq2[:], B.ones[:], sq[:, k % 2, TP:T], start=k == 0, stop=k == KD - 1).then_inc(summed, 1)

            def transposes(u):
                c, kind, ch, t, h = units[u]
                t0, n = TILES[t]
                s = slot[u] % NSTG
                i = trans[u]
                pe.wait_ge(*ready(u))
                if i >= 2:
                    pe.wait_ge(tr_evac, i - 1)
                if kind == "kv" and ch > 0 and t < 4:
                    srcs = [dup[0:n, g, :, :].rearrange("p x d -> p (x d)") for g in range(4)]
                elif kind == "kv" and ch > 0:
                    srcs = [stg[0:n, s, j * P:(j + 1) * P] for j in range(2)]
                elif kind == "q" and t == 4:
                    srcs = [dup[0:n, j, :, :].rearrange("p x d -> p (x d)") for j in range(GRP)]
                else:
                    srcs = [stg[0:n, s, j * P:(j + 1) * P] for j in range(4)]
                for j, src in enumerate(srcs):
                    last = nc.tensor.transpose(tr[:, i % 2, j * P:j * P + n], src, B.ident[0:n, 0:n])
                last.then_inc(tr_done, 1)

            pe.wait_ge(normed, KD)
            prev = None
            for u, (c, kind, ch, t, h) in enumerate(units):
                if u == 0 or units[u - 1][0] != c:
                    pe.wait_ge(w_in_sem[c % 2], 32 * (c // 2 + 1))
                if u >= NM:
                    pe.wait_ge(evac, u - NM + 1)
                for k in range(KD):
                    if kind == "u":
                        cols = slice(h * T // 2, (h + 1) * T // 2)
                        out = mm[:, u % NM, 0:cols.stop - cols.start]
                        last = nc.tensor.matmul(out, B.wb[:, c % 2, k, t * P:(t + 1) * P], B.feat[:, k, cols],
                                                start=k == 0, stop=k == KD - 1)
                    else:
                        t0, n = TILES[t]
                        w = NGATE if kind == "if" else CH
                        last = nc.tensor.matmul(mm[0:n, u % NM, 0:w], B.feat[:, k, t0:t0 + n], B.wb[:, c % 2, k, 0:w],
                                                start=k == 0, stop=k == KD - 1)
                last.then_inc(mm_done, 1)
                if prev is not None and prev in trans:
                    transposes(prev)
                prev = u
            if prev in trans:
                transposes(prev)

        @block.scalar
        def _(act):
            s_ = nc.scalar
            s_.preload_act_table_set("natural_log_exp_and_others")
            act.wait_ge(x_in, 16)
            for k in range(KD):
                if k >= 2:
                    act.wait_ge(summed, k - 1)
                s_.activation(sq[:, k % 2, :], B.feat[:, k, :], ACT.Square).then_inc(squared, 1)
            act.wait_ge(summed, KD)
            s_.activation(rstd[:, 0:TP], ssq[:], ACT.Ln, bias=B.eps[:, 0:1], scale=1.0 / D)
            step = Chain(act, act_step)
            step(s_.activation(rstd[:, TP:T], ssq2[:], ACT.Ln, bias=B.eps[:, 0:1], scale=1.0 / D))
            s_.activation(rstd[:], rstd[:], ACT.Exp, scale=-0.5).then_inc(rs_ready, 1)

            def transposed(u):
                c, kind, ch, t, h = units[u]
                t0, n = TILES[t]
                i = trans[u]
                src = tr[:, i % 2, :]
                act.wait_ge(tr_done, i + 1)
                if kind == "kv" and ch == 0:
                    for cc in range(2):
                        for gp in range(2):
                            blk = src[:, (cc * 2 + gp) * P:(cc * 2 + gp + 1) * P]
                            for jj in range(2):
                                for g2 in range(2):
                                    dst = B.cmpin[64 * jj:64 * jj + 64, t, :].rearrange(
                                        "p (k c n g) -> p c g n k", k=8, c=2, n=8)[:, cc, gp * 2 + g2, :, :]
                                    sv = blk[64 * g2:64 * g2 + 64, :].rearrange("p (n k j) -> p j n k", n=8, k=8)[:, jj, :, :]
                                    last = s_.activation(dst, sv, ACT.Copy)
                elif kind == "kv":
                    kt, new = (B.ksel, B.ksel_new) if ch == 1 else (B.kwin, B.kwin_new)
                    if t < 4:
                        last = s_.activation(kt[:, :, t0:t0 + n], src.rearrange("p (g t) -> p g t", g=4), ACT.Copy)
                    else:
                        last = s_.activation(new[:, :, :], src.rearrange("p (g t) -> p g t", g=4)[:, 0:2, 0:n], ACT.Copy)
                elif t < 4:
                    last = s_.activation(B.qT[:, 4 * ch:4 * ch + 4, t0:t0 + n], src.rearrange("p (h t) -> p h t", h=4),
                                         ACT.Copy, scale=B.qnw[:, 0:1])
                else:
                    for g2 in range(2):
                        half = slice(64 * g2, 64 * g2 + 64)
                        for j in range(GRP):
                            dst = B.qblk[half, ch, :, g2 * 32 + j * TS:g2 * 32 + (j + 1) * TS]
                            last = s_.activation(dst, src[half, j * P:j * P + n].rearrange("p (b t) -> p b t", t=TS),
                                                 ACT.Copy, scale=B.qnw[half, 0:1])
                last.then_inc(tr_evac, 1)

            prev = None
            outs = 0
            for u, (c, kind, ch, t, h) in enumerate(units):
                n = TILES[t][1] if kind != "u" else P
                if u in slot and slot[u] >= NSTG:
                    old = user[slot[u] - NSTG]
                    act.wait_ge(*ready(old))
                    if old in outdma:
                        act.wait_ge(out_sem[slot[u] % NSTG], 16 * (slot_outs(units, slot, outdma, old, NSTG)))
                    if old in trans:
                        act.wait_ge(tr_done, trans[old] + 1)
                act.wait_ge(mm_done, u + 1)
                src = mm[0:n, u % NM, :]
                if kind == "u":
                    f = 4 * ch + t
                    first = T // 2
                    if h == 0:
                        dst, src = B.upad[:, f, CONV - 1:CONV - 1 + first], mm[0:n, u % NM, 0:first]
                    else:
                        s_.activation(B.upad[:, f, CONV - 1 + first:PADW], mm[0:n, u % NM, 0:TP - first], ACT.Copy)
                        dst = B.upad[:, f, PADW:].rearrange("p (b x) -> p b x", x=SPAD)[:, :, CONV - 1:SPAD]
                        src = mm[0:n, u % NM, TP - first:T - first].rearrange("p (b x) -> p b x", x=TS)
                    s_.activation(dst, src, ACT.Copy).then_inc(evac, 1)
                elif kind == "if":
                    s_.activation(B.graw[0:n, t, :], mm[0:n, u % NM, 0:NGATE], ACT.Copy).then_inc(evac, 1)
                elif kind in ("kv", "q"):
                    s_.activation(stg[0:n, slot[u] % NSTG, :], src, ACT.Copy).then_inc(evac, 1)
                    if kind == "q" or ch > 0:
                        nh = 8 if kind == "q" else 4
                        act.wait_ge(ms_ready, 1 + sum(1 for v in range(u) if units[v][1] == "q" or (units[v][1] == "kv" and units[v][2] > 0)))
                        step(s_.activation(ms[0:n, 0:nh], ms[0:n, 0:nh], ACT.Ln, bias=B.eps[0:n, 0:1], scale=1.0 / AD))
                        s_.activation(ms[0:n, 0:nh], ms[0:n, 0:nh], ACT.Exp, scale=-0.5).then_inc(rstd_ready, 1)
                else:
                    act.wait_ge(unit_ready, vec_count[u] - 1)
                    if kind != "o":
                        s_.activation(stg[0:n, slot[u] % NSTG, :], src, ACT.Copy)
                    s_.activation(stg2[0:n, :], src, ACT.Exp, scale=-1.0).then_inc(evac, 1)
                if prev is not None and prev in trans:
                    transposed(prev)
                prev = u
            if prev in trans:
                transposed(prev)

        @block.vector
        def _(dve):
            v = nc.vector
            step = Chain(dve, dve_step)
            dve.wait_ge(rs_ready, 1)
            for k in range(KD):
                v.scalar_tensor_tensor(B.feat[:, k, :], B.feat[:, k, :], B.normw[:, k:k + 1], rstd[:],
                                       ALU.mult, ALU.mult).then_inc(normed, 1)
            step(v.memset(B.qblk[:].rearrange("p a b c -> p (a b c)"), 0.0))
            norms = 0
            for u, (c, kind, ch, t, h) in enumerate(units):
                n = TILES[t][1]
                dve.wait_ge(evac, u + 1)
                if u not in vec_count:
                    continue
                s = slot[u] % NSTG
                if kind == "q" or (kind == "kv" and ch > 0):
                    nh = 8 if kind == "q" else 4
                    x = stg[0:n, s, 0:nh * AD]
                    x3 = x.rearrange("p (h d) -> p h d", d=AD)
                    step(v.tensor_tensor(msq[0:n, 0:nh * AD], x, x, ALU.mult))
                    v.tensor_reduce(ms[0:n, 0:nh], msq[0:n, 0:nh * AD].rearrange("p (h d) -> p h d", d=AD), AX,
                                    ALU.add).then_inc(ms_ready, 1)
                    norms += 1
                    dve.wait_ge(rstd_ready, norms)
                    if kind == "q" and t == 4:
                        dve.wait_ge(tr_done, dup_free(u))
                        scaled = v.tensor_tensor(
                            dup[0:n].rearrange("p a g d -> p g a d"), x.rearrange("p (g a d) -> p g a d", g=2, a=GRP),
                            ms[0:n, 0:nh].rearrange("p (g a) -> p g a", g=2).unsqueeze(3).to_broadcast([n, 2, GRP, AD]),
                            ALU.mult)
                    else:
                        scaled = v.tensor_tensor(x3, x3, ms[0:n, 0:nh].unsqueeze(2).to_broadcast([n, nh, AD]), ALU.mult)
                if kind == "kv":
                        step(scaled)
                        step(v.tensor_tensor(x3, x3, B.knw[0:n, ch * AD:(ch + 1) * AD].unsqueeze(1).to_broadcast([n, KV, AD]),
                                             ALU.mult))
                        vdst = (B.vsel, B.vsel_new) if ch == 1 else (B.vwin, B.vwin_new)
                        vd = vdst[0][:, t, :] if t < 4 else vdst[1][:, :]
                        last = v.tensor_copy(vd, stg[0:n, s, 256:512])
                        if t < 4:
                            if dup_free(u):
                                dve.wait_ge(tr_done, dup_free(u))
                            step(last)
                            step(v.tensor_copy(dup[0:n, :, 0, :], x3))
                            last = v.tensor_copy(dup[0:n, :, 1, :], x3)
                        last.then_inc(unit_ready, 1)
                elif kind == "q":
                    scaled.then_inc(unit_ready, 1)
                else:
                    step(v.tensor_scalar(stg2[0:n, :], stg2[0:n, :], 1.0, None, ALU.add))
                    if kind == "o":
                        v.reciprocal(stg[0:n, s, :], stg2[0:n, :]).then_inc(unit_ready, 1)
                    else:
                        step(v.reciprocal(stg2[0:n, :], stg2[0:n, :]))
                        v.tensor_tensor(stg[0:n, s, :], stg[0:n, s, :], stg2[0:n, :], ALU.mult).then_inc(unit_ready, 1)


def gate_rows(nc, B, a, o):
    with Semaphores(nc) as sem, ExitStack() as ctx:
        sb = lambda n, s, d=F32: ctx.enter_context(nc.sbuf_tensor(n, s, d))
        ps = lambda n, s: ctx.enter_context(nc.psum_tensor(n, s, F32))
        gi, gf, gneg = sb("g_li", [MH, T]), sb("g_lf", [MH, T]), sb("g_abs", [MH, T])
        gb, gg, gmax = sb("g_b", [MH, T]), sb("g_g", [MH, T]), sb("g_max", [MH, T])
        rm, rw, rdec = sb("g_m", [MH, T]), sb("g_w", [MH, T]), sb("g_dec", [MH, TSA])
        hist = sb("conv_hist", [P, 8, NB, CONV - 1])
        last_u = sb("last_u", [P, 8, (1 + NB) * (CONV - 1)])
        rows_u = sb("rows_u", [(1 + NB) * (CONV - 1), MW])
        pI, pF, pS = ps("g_pi", [MH, TP]), ps("g_pf", [MH, TP]), ps("g_ps", [MH, 2, TSA])
        pcol = ps("g_pcol", [P, 5, 4, MH])
        pb = ps("g_pb", [P, 2, CH])
        pu = ps("g_pu", [(1 + NB) * (CONV - 1), 2, CH])
        loaded, gates_t = sem("g_loaded"), sem("gates_t")
        rows_ready, cols_t, spread = sem("rows_ready"), sem("cols_t"), sem("spread")
        spread_used = sem("spread_used")
        abs_ready, ln_ready, stored = sem("abs_ready"), sem("ln_ready"), sem("g_stored")
        u_packed, u_t, u_rows = sem("u_packed"), sem("u_t"), sem("u_rows")
        dve_step, act_step, sig_ready = sem("g_dve"), sem("g_act"), sem("sig_exp")
        NH3 = (1 + NB) * (CONV - 1)
        block = ctx.enter_context(nc.Block())
        ends = lambda r: r[:, TP:T].rearrange("p (b t) -> p b t", t=TS)

        @block.sync
        def _(sp):
            sp.dma_start(hist[:], a["conv_state"]).then_inc(loaded, 16)
            sp.wait_ge(rows_ready, 1)
            with nc.allow_non_contiguous_dma("a column of each row"):
                sp.dma_start(o["m_prompt"], rm[:, TP - 1:TP]).then_inc(stored, 16)
                sp.dma_start(o["m_sample"], ends(rm)[:, :, TS - 1]).then_inc(stored, 16)
            sp.wait_ge(u_rows, 2)
            sp.dma_start(o["conv_prompt"], rows_u[0:CONV - 1, :]).then_inc(stored, 16)
            sp.dma_start(o["conv_sample"].rearrange("b j n -> (b j) n"), rows_u[CONV - 1:NH3, :]).then_inc(stored, 16)
            sp.wait_ge(stored, 64)

        @block.tensor
        def _(pe):
            for t, (t0, n) in enumerate(TILES):
                for w in range(2):
                    dst = (pI, pF)[w][:, t0:t0 + n] if t < 4 else pS[:, w, 0:n]
                    last = nc.tensor.transpose(dst, B.graw[0:n, t, w * MH:(w + 1) * MH], B.ident[0:n, 0:n])
            last.then_inc(gates_t, 1)
            pe.wait_ge(u_packed, 1)
            for f in range(8):
                last = nc.tensor.transpose(pu[:, f // 4, (f % 4) * P:(f % 4 + 1) * P], last_u[:, f, :], B.ident[:])
            last.then_inc(u_t, 1)
            pe.wait_ge(rows_ready, 1)
            for t, (t0, n) in enumerate(TILES):
                for w, r in enumerate((gg, rm, rw)):
                    last = nc.tensor.transpose(pcol[0:n, t, w, :], r[:, t0:t0 + n], B.ident[0:MH, 0:MH])
            last = nc.tensor.transpose(pcol[0:TSA, 4, 3, :], rdec[:], B.ident[0:MH, 0:MH])
            last.then_inc(cols_t, 1)
            for h in range(MH):
                if h:
                    pe.wait_ge(spread_used, h)
                nc.tensor.matmul(pb[:, 0, :], B.headsel[:, h, :], gmax[:, 0:TP], start=True, stop=True)
                nc.tensor.matmul(pb[:, 1, 0:TSA], B.headsel[:, h, :], gmax[:, TP:T], start=True, stop=True)
                nc.tensor.matmul(pb[:, 1, TSA:TSA + NB], B.headsel[:, h, :],
                                 rdec[:].rearrange("p (b t) -> p b t", t=TS)[:, :, TS - 1],
                                 start=True, stop=True).then_inc(spread, 1)

        @block.scalar
        def _(act):
            s_ = nc.scalar
            step = Chain(act, act_step)
            step(s_.activation(B.gsig[:, 0:4, :], B.graw[:, 0:4, 2 * MH:NGATE], ACT.Exp, scale=-1.0))
            s_.activation(B.gsig[0:TSA, 4, :], B.graw[0:TSA, 4, 2 * MH:NGATE], ACT.Exp, scale=-1.0).then_inc(sig_ready, 1)
            act.wait_ge(abs_ready, 1)
            step(s_.activation(gneg[:], gneg[:], ACT.Exp, scale=-1.0))
            s_.activation(gneg[:], gneg[:], ACT.Ln, bias=1.0).then_inc(ln_ready, 1)
            act.wait_ge(u_t, 1)
            for i in range(2):
                s_.activation(rows_u[:, i * CH:(i + 1) * CH], pu[:, i, :], ACT.Copy).then_inc(u_rows, 1)
            act.wait_ge(cols_t, 1)
            s_.activation(B.cols[:, 0:4, 0, :], pcol[:, 0:4, 0, :], ACT.Copy)
            s_.activation(B.cols[0:TSA, 4, 0, :], pcol[0:TSA, 4, 0, :], ACT.Copy)
            s_.activation(B.cols[:, 0:4, 1, :], pcol[:, 0:4, 1, :], ACT.Exp, scale=-1.0)
            s_.activation(B.cols[0:TSA, 4, 1, :], pcol[0:TSA, 4, 1, :], ACT.Exp, scale=-1.0)
            s_.activation(B.cols[:, 0:4, 2, :], pcol[:, 0:4, 2, :], ACT.Exp)
            s_.activation(B.cols[0:TSA, 4, 2:4, :], pcol[0:TSA, 4, 2:4, :], ACT.Exp)
            for h in range(MH):
                act.wait_ge(spread, h + 1)
                s_.activation(B.mbc[:, h, 0:TP], pb[:, 0, :], ACT.Copy)
                s_.activation(B.mbc[:, h, TP:T], pb[:, 1, 0:TSA], ACT.Copy)
                s_.activation(B.decbc[:, h, :], pb[:, 1, TSA:TSA + NB], ACT.Exp).then_inc(spread_used, 1)

        @block.vector
        def _(dve):
            v = nc.vector
            step = Chain(dve, dve_step)
            step(v.memset(B.upad[:, :, 0:CONV - 1], 0.0))
            dve.wait_ge(loaded, 16)
            for f in range(8):
                w = B.upad[:, f, PADW:].rearrange("p (b x) -> p b x", x=SPAD)
                v.tensor_copy(w[:, :, 0:CONV - 1], hist[:, f, :, :])
                v.tensor_copy(last_u[:, f, CONV - 1:].rearrange("p (b j) -> p b j", j=CONV - 1), w[:, :, TS:SPAD])
            v.tensor_copy(last_u[:, :, 0:CONV - 1], B.upad[:, :, TP:PADW]).then_inc(u_packed, 1)
            dve.wait_ge(gates_t, 1)
            v.tensor_scalar(gi[:, 0:TP], pI[:], B.bif[:, 0:1], None, ALU.add)
            v.tensor_scalar(gi[:, TP:T], pS[:, 0, :], B.bif[:, 0:1], None, ALU.add)
            v.tensor_scalar(gf[:, 0:TP], pF[:], B.bif[:, 1:2], None, ALU.add)
            step(v.tensor_scalar(gf[:, TP:T], pS[:, 1, :], B.bif[:, 1:2], None, ALU.add))
            step(v.tensor_scalar(gneg[:], gf[:], -1.0, None, ALU.mult))
            v.tensor_tensor(gneg[:], gneg[:], gf[:], ALU.max).then_inc(abs_ready, 1)
            step(v.tensor_scalar(gf[:], gf[:], 0.0, None, ALU.min))
            dve.wait_ge(ln_ready, 1)
            step(v.tensor_tensor(gf[:], gf[:], gneg[:], ALU.subtract))
            step(v.tensor_tensor_scan(gb[:], B.keep[:], gf[:], 0.0, ALU.mult, ALU.add))
            step(v.tensor_tensor(gg[:], gi[:], gb[:], ALU.subtract))
            step(v.tensor_copy(gi[:], gg[:]))
            step(v.tensor_tensor(ends(gi)[:, :, 0], ends(gg)[:, :, 0], B.m0[:], ALU.max))
            step(v.tensor_tensor_scan(gmax[:], B.restart[:], gi[:], NEG, ALU.add, ALU.max))
            step(v.tensor_tensor(rm[:], gb[:], gmax[:], ALU.add))
            step(v.tensor_scalar(rw[:, 0:TP], gg[:, 0:TP], gmax[:, TP - 1:TP], None, ALU.subtract))
            step(v.tensor_tensor(ends(rw), ends(gg), ends(gmax)[:, :, TS - 1:TS].to_broadcast([MH, NB, TS]), ALU.subtract))
            v.tensor_tensor(rdec[:].rearrange("p (b t) -> p b t", t=TS), B.m0[:].unsqueeze(2).to_broadcast([MH, NB, TS]),
                            ends(gmax), ALU.subtract).then_inc(rows_ready, 1)
            dve.wait_ge(sig_ready, 1)
            for part in (B.gsig[:, 0:4, :], B.gsig[0:TSA, 4, :]):
                step(v.tensor_scalar(part, part, 1.0, None, ALU.add))
                step(v.reciprocal(part, part))


def mlstm_heads(nc, B, a, o):
    MD1 = MD + 1
    with ExitStack() as ctx:
        sb = lambda n, s, d=F32: ctx.enter_context(nc.sbuf_tensor(n, s, d))
        ps = lambda n, s: ctx.enter_context(nc.psum_tensor(n, s, F32))
        taken = [0]

        def carve(shape, parts=P):
            size = int(np.prod(shape))
            flat = B.wide[0:parts, taken[0]:taken[0] + size]
            taken[0] += size
            names = "abc"[:len(shape)]
            return flat.rearrange(f"p ({' '.join(names)}) -> p {' '.join(names)}", **dict(zip(names, shape)))

        wq, wk, wv = (sb(n, [P, 2, MD]) for n in ("m_wq", "m_wk", "m_wv"))
        state = carve([NB, 2, MD1])
        sgo, sgz = carve([5, MD]), carve([5, MD])
        mnw = sb("m_normw", [P, MW])
        cacc, ch, uh = carve([2, T]), carve([2, T]), carve([2, T])
        qh, kh = carve([2, T]), carve([2, T])
        qz = sb("m_qz", [P, 2, NB * (TSA + TS)])
        kw, kwz = carve([5, MD]), carve([NB, MD], TSA)
        vh = sb("m_v", [P, 5, MD1])
        wgt, wgts = sb("m_weights", [P, 4, TP]), sb("m_weights_s", [TSA, TSA])
        col = sb("m_cols", [P, 5, 4])
        hv, hsq = sb("m_hv", [P, 5, MD]), sb("m_hsq", [P, MD])
        hms, rden = sb("m_ms", [P, 5]), sb("m_rden", [P, 5])
        inter, nums = sb("m_inter", [TSA, MD1]), sb("m_nums", [TSA, MD1])
        cst = sb("m_cst", [P, 2, MD1])
        pj = ps("m_pj", [P, 3, CH])
        st = ps("m_st", [P, 2, CH])
        nm = ps("m_nm", [P, 2, CH])
        with Semaphores(nc) as sem, nc.Block() as block:
            const_ready = sem("m_const")

            @block.sync
            def _(sp):
                sp.dma_start(mnw[:], a["m_norm_w"].partition_broadcast(P)).then_inc(const_ready, 16)
                sp.wait_ge(const_ready, 16)

            @block.vector
            def _(dve):
                nc.vector.memset(qz[:], 0.0)
                nc.vector.memset(vh[:, :, MD:MD1], 1.0)

        with nc.Fori(0, MH) as h, Semaphores(nc) as sem, ExitStack() as turn:
            w_loaded, loaded, conv_ready, conv_exp, ch_ready, u_ready = (sem(n) for n in ("m_w_loaded", "m_loaded", "conv_ready", "conv_exp", "ch_ready", "u_ready"))
            pj_done, pj_act, pj_dve = sem("pj_done"), sem("pj_act"), sem("pj_dve")
            arg_ready, e_ready, e_masked = sem("arg_ready"), sem("e_ready"), sem("e_masked")
            qz_ready, kwz_ready = sem("qz_ready"), sem("kwz_ready")
            st_done, st_used, nm_done, nm_used = sem("st_done"), sem("st_used"), sem("nm_done"), sem("nm_used")
            hv_ready, rms_ready, h_ready, cs_ready, cp_ready = (sem(n) for n in ("hv_ready", "rms_ready", "h_ready", "cs_ready", "cp_ready"))
            stored = sem("m_stored")
            dve_step, act_step = sem("m_dve_step"), sem("m_act_step")
            LOADS = NB + 4
            STORES = 5 + 2 + 2 * NB
            RING = 33
            ACT_UNITS = [0, 1, 2, 3, 9, 10, 11, 12, 13, 14, 15, 16]
            DVE_UNITS = [4, 5, 6, 7, 8] + list(range(17, 33))
            order = ["S0", "S1", "N0", "S2", "N1", "S3", "S4", "N2", "N3", "I", "N4"]
            block = turn.enter_context(nc.Block())

            @block.sync
            def _(sp):
                hh = bass.ds(h, 1)
                for dst, src in ((wq, "wq"), (wk, "wk"), (wv, "wv")):
                    sp.dma_start(dst[:], a[src][hh].rearrange("x (k p) n -> p (x k) n", p=P)).then_inc(w_loaded, 16)
                for dst, w in ((sgo, 0), (sgz, 1)):
                    cols = bass.ds(h * MD, MD)
                    sp.dma_start(dst[:, 0:4, :], B.gates_dram[w, 0:TP, cols].rearrange("(t p) n -> p t n", p=P)).then_inc(loaded, 16)
                    sp.dma_start(dst[0:TSA, 4, :], B.gates_dram[w, TP:T, cols]).then_inc(loaded, 16)
                for b in range(NB):
                    sp.dma_start(state[:, b, :, :], a["state"][b, hh].rearrange("x (k p) n -> p (x k) n", p=P)).then_inc(loaded, 16)
                for t, (t0, n) in enumerate(TILES):
                    sp.wait_ge(h_ready, t + 1)
                    sp.dma_start(B.cat_dram[t0:t0 + n, bass.ds(h * MD, MD)], hv[0:n, t, :]).then_inc(stored, 16)
                sp.wait_ge(cp_ready, 1)
                with nc.allow_non_contiguous_dma("the normaliser is one column"):
                    sp.dma_start(o["C_prompt"][hh].rearrange("x (k p) n -> p (x k) n", p=P), cst[:, :, 0:MD]).then_inc(stored, 16)
                    sp.dma_start(o["n_prompt"][hh].rearrange("x (k p) -> p (x k)", p=P), cst[:, :, MD]).then_inc(stored, 16)
                    for b in range(NB):
                        sp.wait_ge(cs_ready, b + 1)
                        sp.dma_start(o["C_sample"][b, hh].rearrange("x (k p) n -> p (x k) n", p=P), state[:, b, :, 0:MD]).then_inc(stored, 16)
                        sp.dma_start(o["n_sample"][b, hh].rearrange("x (k p) -> p (x k)", p=P), state[:, b, :, MD]).then_inc(stored, 16)
                sp.wait_ge(stored, 16 * STORES)

            @block.tensor
            def _(pe):
                pe.wait_ge(w_loaded, 48)
                pe.wait_ge(ch_ready, 1)
                pe.wait_ge(u_ready, 1)
                r = 0

                def free(r):
                    if r >= 3:
                        q = r - 3
                        if q in ACT_UNITS:
                            pe.wait_ge(pj_act, ACT_UNITS.index(q) + 1)
                        else:
                            pe.wait_ge(pj_dve, DVE_UNITS.index(q) + 1)

                for w in (wq, wk):
                    for dt in range(2):
                        free(r)
                        cols = slice(dt * P, (dt + 1) * P)
                        for kt in range(2):
                            nc.tensor.matmul(pj[:, r % 3, :], w[:, kt, cols], ch[:, kt, 0:TP], start=kt == 0, stop=kt == 1)
                        if r >= 2:
                            pe.wait_ge(pj_act, r - 1)
                        for kt in range(2):
                            last = nc.tensor.matmul(nm[:, r % 2, 0:TSA], w[:, kt, cols], ch[:, kt, TP:T], start=kt == 0, stop=kt == 1)
                        last.then_inc(pj_done, 1)
                        r += 1
                for w, x in ((wk, ch), (wv, uh)):
                    for t0, n in TILES:
                        free(r)
                        for kt in range(2):
                            last = nc.tensor.matmul(pj[0:n, r % 3, 0:MD], x[:, kt, t0:t0 + n], w[:, kt, :], start=kt == 0, stop=kt == 1)
                        last.then_inc(pj_done, 1)
                        r += 1
                si = ni = 0
                for what in order:
                    if what[0] == "S":
                        i = int(what[1])
                        if i == 0:
                            pe.wait_ge(pj_act, 4)
                        if si >= 2:
                            pe.wait_ge(st_used, si - 1)
                        for kt in range(2):
                            if i < 4:
                                last = nc.tensor.matmul(st[:, si % 2, 0:TP - i * P], kh[:, kt, i * P:(i + 1) * P],
                                                        qh[:, kt, i * P:TP], start=kt == 0, stop=kt == 1)
                            else:
                                last = nc.tensor.matmul(st[0:TSA, si % 2, 0:TSA], kh[:, kt, TP:T], qh[:, kt, TP:T],
                                                        start=kt == 0, stop=kt == 1)
                        last.then_inc(st_done, 1)
                        si += 1
                    elif what[0] == "N":
                        j = int(what[1])
                        if j == 0:
                            pe.wait_ge(pj_act, 9)
                        pe.wait_ge(st_used, j + 1)
                        if ni >= 2:
                            pe.wait_ge(nm_used, ni - 1)
                        if j < 4:
                            for i in range(j + 1):
                                last = nc.tensor.matmul(nm[:, ni % 2, 0:MD1], wgt[:, i, j * P:(j + 1) * P], vh[:, i, :],
                                                        start=i == 0, stop=i == j)
                        else:
                            last = nc.tensor.matmul(nm[0:TSA, ni % 2, 0:MD1], wgts[:], vh[0:TSA, 4, :], start=True, stop=True)
                        last.then_inc(nm_done, 1)
                        ni += 1
                    else:
                        pe.wait_ge(loaded, 16 * LOADS)
                        pe.wait_ge(qz_ready, 1)
                        free(r)
                        for b in range(NB):
                            for kt in range(2):
                                last = nc.tensor.matmul(pj[0:TSA, r % 3, 0:MD1], qz[:, kt, b * TSA:(b + 1) * TSA], state[:, b, kt, :],
                                                        start=b + kt == 0, stop=b + kt == NB)
                        last.then_inc(pj_done, 1)
                        r += 1
                for dt in range(2):
                    free(r)
                    for i in range(4):
                        last = nc.tensor.matmul(pj[:, r % 3, 0:MD1], kw[:, i, dt * P:(dt + 1) * P], vh[:, i, :], start=i == 0, stop=i == 3)
                    last.then_inc(pj_done, 1)
                    r += 1
                pe.wait_ge(kwz_ready, 1)
                for b in range(NB):
                    for dt in range(2):
                        free(r)
                        nc.tensor.matmul(pj[:, r % 3, 0:MD1], kwz[:, b, dt * P:(dt + 1) * P], vh[0:TSA, 4, :],
                                         start=True, stop=True).then_inc(pj_done, 1)
                        r += 1
                assert r == RING

            @block.scalar
            def _(act):
                s_ = nc.scalar
                step = Chain(act, act_step)
                act.wait_ge(conv_ready, 1)
                step(s_.activation(ch[:], cacc[:], ACT.Exp, scale=-1.0))
                step(s_.activation(ch[:], ch[:], ACT.Ln, bias=1.0))
                s_.activation(ch[:], ch[:], ACT.Exp, scale=-1.0).then_inc(conv_exp, 1)

                def unit(r):
                    act.wait_ge(pj_done, r + 1)

                for r in range(4):
                    unit(r)
                    dst, sc = (qh, 1.0) if r < 2 else (kh, 1.0 / 16)
                    s_.activation(dst[:, r % 2, 0:TP], pj[:, r % 3, :], ACT.Copy, scale=sc)
                    s_.activation(dst[:, r % 2, TP:T], nm[:, r % 2, 0:TSA], ACT.Copy, scale=sc).then_inc(pj_act, 1)
                for i in range(5):
                    act.wait_ge(arg_ready, i + 1)
                    w = wgt[:, i, i * P:TP] if i < 4 else wgts[:]
                    s_.activation(w, w, ACT.Exp, scale=-1.0).then_inc(e_ready, 1)
                for t, (t0, n) in enumerate(TILES):
                    unit(9 + t)
                    s_.activation(vh[0:n, t, 0:MD], pj[0:n, (9 + t) % 3, 0:MD], ACT.Copy).then_inc(pj_act, 1)
                for j in range(5):
                    n = TILES[j][1]
                    if j == 4:
                        unit(14)
                        s_.activation(inter[:], pj[0:TSA, 14 % 3, 0:MD1], ACT.Copy, scale=col[0:TSA, 4, 3:4]).then_inc(pj_act, 1)
                    act.wait_ge(hv_ready, j + 1)
                    step(s_.activation(hsq[0:n, :], hv[0:n, j, :], ACT.Square, accum_out=hms[0:n, j:j + 1]))
                    step(s_.activation(hms[0:n, j:j + 1], hms[0:n, j:j + 1], ACT.Ln, bias=B.eps[0:n, 0:1], scale=1.0 / MD))
                    s_.activation(hms[0:n, j:j + 1], hms[0:n, j:j + 1], ACT.Exp, scale=-0.5).then_inc(rms_ready, 1)
                for dt in range(2):
                    unit(15 + dt)
                    last = s_.activation(cst[:, dt, :], pj[:, (15 + dt) % 3, 0:MD1], ACT.Copy)
                    if dt == 0:
                        last.then_inc(pj_act, 1)
                last.then_inc(pj_act, 1)
                act.wait_ge(pj_act, len(ACT_UNITS))
                s_.activation(hsq[:, 0:1], hsq[:, 0:1], ACT.Copy).then_inc(cp_ready, 1)

            @block.gpsimd
            def _(pool):
                g = nc.gpsimd
                ft = bass.ds(h * 2, 2)
                g.tensor_copy(uh[:, :, 0:TP], B.upad[:, ft, CONV - 1:PADW])
                for kt in range(2):
                    sv = B.upad[:, bass.ds(h * 2 + kt, 1), PADW:].rearrange("p f (b x) -> p (f b) x", x=SPAD)[:, :, CONV - 1:SPAD]
                    last = g.tensor_copy(uh[:, kt, TP:T].rearrange("p (b x) -> p b x", x=TS), sv)
                last.then_inc(u_ready, 1)
                for i in range(4):
                    pool.wait_ge(e_ready, i + 1)
                    w = wgt[:, i, i * P:(i + 1) * P]
                    g.affine_select(out=w, in_=w, compare_op=ALU.is_ge, fill=0.0, base=0, pattern=[[1, P]],
                                    channel_multiplier=-1).then_inc(e_masked, 1)

            @block.vector
            def _(dve):
                v = nc.vector
                step = Chain(dve, dve_step)
                for kt in range(2):
                    f = bass.ds(h * 2 + kt, 1)
                    for sample in range(2):
                        if sample:
                            dst = cacc[:, kt, TP:T].rearrange("p (b x) -> p b x", x=TS)
                            tap = lambda j: B.upad[:, f, PADW:].rearrange("p f (b x) -> p (f b) x", x=SPAD)[:, :, j:j + TS]
                        else:
                            dst = cacc[:, kt, 0:TP]
                            tap = lambda j: B.upad[:, f, j:j + TP].rearrange("p f x -> p (f x)")
                        if not sample:
                            step(v.tensor_copy(col[:, kt, :], B.convw[:, f, :].rearrange("p f x -> p (f x)")))
                            step(v.tensor_copy(rden[:, kt:kt + 1], B.convb[:, f]))
                        step(v.tensor_scalar(dst, tap(0), col[:, kt, 0:1], rden[:, kt:kt + 1], ALU.mult, ALU.add))
                        for j in range(1, CONV):
                            last = v.scalar_tensor_tensor(dst, tap(j), col[:, kt, j:j + 1], dst, ALU.mult, ALU.add)
                            if j < CONV - 1:
                                step(last)
                        if (kt, sample) != (1, 1):
                            step(last)
                last.then_inc(conv_ready, 1)
                dve.wait_ge(conv_exp, 1)
                v.tensor_tensor(ch[:], ch[:], cacc[:], ALU.mult).then_inc(ch_ready, 1)
                step(v.tensor_copy(col[:, 0:4, 0:3], B.cols[:, 0:4, 0:3, bass.ds(h, 1)].rearrange("p t w x -> p t (w x)")))
                step(v.tensor_copy(col[0:TSA, 4, :], B.cols[0:TSA, 4, :, bass.ds(h, 1)].rearrange("p w x -> p (w x)")))
                for i in range(4):
                    v.tensor_scalar(wgt[:, i, i * P:TP], B.mbc[:, bass.ds(h, 1), i * P:TP].rearrange("p x t -> p (x t)"),
                                    col[:, i, 0:1], 0.0, ALU.subtract, ALU.max).then_inc(arg_ready, 1)
                v.tensor_scalar(wgts[:], B.mbc[0:TSA, bass.ds(h, 1), TP:T].rearrange("p x t -> p (x t)"),
                                col[0:TSA, 4, 0:1], 0.0, ALU.subtract, ALU.max).then_inc(arg_ready, 1)
                for t, (t0, n) in enumerate(TILES):
                    dve.wait_ge(pj_done, 4 + t + 1)
                    v.tensor_scalar(kw[0:n, t, :], pj[0:n, (4 + t) % 3, 0:MD], col[0:n, t, 2:3], 1.0 / 16,
                                    ALU.mult, ALU.mult).then_inc(pj_dve, 1)
                dve.wait_ge(pj_dve, 5)
                for b in range(NB):
                    last = v.tensor_scalar(kwz[:, b, :], kw[0:TSA, 4, :], B.member[:, b:b + 1], None, ALU.mult)
                last.then_inc(kwz_ready, 1)
                dve.wait_ge(pj_act, 2)
                for kt in range(2):
                    last = v.tensor_copy(qz[:, kt, :].rearrange("p (b x) -> p b x", x=TSA + TS)[:, :, 0:TS],
                                         qh[:, kt, TP:T].rearrange("p (b x) -> p b x", x=TS))
                last.then_inc(qz_ready, 1)
                dve.wait_ge(loaded, 16 * LOADS)
                si = ni = 0
                for what in order:
                    if what[0] == "S":
                        i = int(what[1])
                        dve.wait_ge(st_done, si + 1)
                        if i < 4:
                            dve.wait_ge(e_masked, i + 1)
                            v.tensor_tensor(wgt[:, i, i * P:TP], st[:, si % 2, 0:TP - i * P], wgt[:, i, i * P:TP],
                                            ALU.mult).then_inc(st_used, 1)
                        else:
                            dve.wait_ge(e_ready, 5)
                            step(v.tensor_tensor(wgts[:], wgts[:], B.blockdiag[:].rearrange("p b t -> p (b t)"), ALU.mult))
                            v.tensor_tensor(wgts[:], st[0:TSA, si % 2, 0:TSA], wgts[:], ALU.mult).then_inc(st_used, 1)
                        si += 1
                    elif what[0] == "N":
                        j = int(what[1])
                        n = TILES[j][1]
                        dve.wait_ge(nm_done, ni + 1)
                        num = nm[0:n, ni % 2, :]
                        if j == 4:
                            dve.wait_ge(pj_act, 10)
                            step(v.tensor_tensor(nums[:], num[:, 0:MD1], inter[:], ALU.add))
                            num = nums[:]
                        step(v.scalar_tensor_tensor(rden[0:n, j:j + 1], num[:, MD:MD1], -1.0, col[0:n, j, 1:2], ALU.mult, ALU.max))
                        step(v.tensor_tensor(rden[0:n, j:j + 1], num[:, MD:MD1], rden[0:n, j:j + 1], ALU.max))
                        step(v.reciprocal(rden[0:n, j:j + 1], rden[0:n, j:j + 1]))
                        v.scalar_tensor_tensor(hv[0:n, j, :], num[:, 0:MD], rden[0:n, j:j + 1], sgo[0:n, j, :],
                                               ALU.mult, ALU.mult).then_inc(hv_ready, 1)
                        dve.wait_ge(hv_ready, ni + 1)
                        v.tensor_copy(rden[0:n, j:j + 1], rden[0:n, j:j + 1]).then_inc(nm_used, 1)
                        dve.wait_ge(rms_ready, ni + 1)
                        step(v.scalar_tensor_tensor(hv[0:n, j, :], hv[0:n, j, :], hms[0:n, j:j + 1],
                                                    mnw[0:n, bass.ds(h * MD, MD)], ALU.mult, ALU.mult))
                        v.tensor_tensor(hv[0:n, j, :], hv[0:n, j, :], sgz[0:n, j, :], ALU.mult).then_inc(h_ready, 1)
                        ni += 1
                for b in range(NB):
                    for dt in range(2):
                        dve.wait_ge(pj_done, 17 + 2 * b + dt + 1)
                        v.scalar_tensor_tensor(state[:, b, dt, :], state[:, b, dt, :], B.decbc[:, bass.ds(h, 1), b],
                                               pj[:, (17 + 2 * b + dt) % 3, 0:MD1], ALU.mult, ALU.add).then_inc(pj_dve, 1)
                    dve.wait_ge(pj_dve, 5 + 2 * b + 2)
                    v.tensor_copy(rden[:, 0:1], rden[:, 0:1]).then_inc(cs_ready, 1)


def compress_prompt(nc, B, a):
    NC = NCMP_P
    with Semaphores(nc) as sem, ExitStack() as ctx:
        sb = lambda n, s, d=F32: ctx.enter_context(nc.sbuf_tensor(n, s, d))
        ps = lambda n, s: ctx.enter_context(nc.psum_tensor(n, s, F32))
        cpe = sb("cp_pe", [P, 2, 2, 8])
        first, second = sb("cp_first", [P, 4 * 32]), sb("cp_second", [P, 4 * 32])
        hid, gate = sb("cp_hid", [P, 4 * NC]), sb("cp_gate", [P, 4 * NC])
        hidg = sb("cp_hidg", [P, KV, NC])
        sq, ms = sb("cp_sq", [32, KV, AD]), sb("cp_ms", [32, KV])
        kdup = sb("cp_kdup", [32, KV, 2, AD])
        pbias, ph, pk, pv, pt = ps("cp_pbias", [P, 1]), ps("cp_ph", [P, 2, CH]), ps("cp_pk", [32, KV * AD]), ps("cp_pv", [P, KV * AD]), ps("cp_pt", [P, KV, 32])
        loaded, biased, hid_done, split, summed_up, exp_done, hid_ready = (sem(n) for n in (
            "cp_loaded", "cp_biased", "cp_hid_done", "cp_split", "cp_summed", "cp_exp", "cp_hid_ready"))
        kv_done, ms_ready, rstd_ready, k_ready, t_done = (sem(n) for n in ("cp_kv", "cp_ms_ready", "cp_rstd", "cp_kready", "cp_t"))
        bias_ready, dve_step, act_step = sem("cp_bias_ready"), sem("cp_dve"), sem("cp_act")
        block = ctx.enter_context(nc.Block())

        @block.sync
        def _(sp):
            sp.dma_start(B.cw1[:], a["cmp_w1"]).then_inc(loaded, 16)
            sp.dma_start(cpe[:], a["cmp_pe"]).then_inc(loaded, 16)
            sp.wait_ge(loaded, 32)

        @block.tensor
        def _(pe):
            pe.wait_ge(loaded, 32)
            for c in range(2):
                for i in range(16):
                    x, k = i // 8, i % 8
                    last = nc.tensor.matmul(pbias[64 * c:64 * c + 64, :], B.cw1[:, c, k, 64 * x:64 * x + 64], cpe[:, c, x, k:k + 1],
                                            start=i == 0, stop=i == 15)
            last.then_inc(biased, 1)
            for c in range(2):
                for k in range(8):
                    last = nc.tensor.matmul(ph[:, c, 0:P], B.cw1[:, c, k, :], B.cmpin[:, :, k * 64 + c * 32:k * 64 + c * 32 + 32],
                                            start=k == 0, stop=k == 7)
                last.then_inc(hid_done, 1)
            pe.wait_ge(hid_ready, 1)
            for g in range(KV):
                nc.tensor.matmul(pk[0:NC, g * AD:(g + 1) * AD], hidg[0:64, g, :], B.cw2[0:64, :], start=True, stop=True)
            for j in range(GRP):
                for g in range(KV):
                    last = nc.tensor.matmul(pv[32 * j:32 * j + NC, g * AD:(g + 1) * AD], hidg[64:128, g, :], B.cw2[64:128, :],
                                            start=True, stop=True)
            last.then_inc(kv_done, 1)
            pe.wait_ge(k_ready, 1)
            for g in range(KV):
                last = nc.tensor.transpose(pt[:, g, 0:NC], kdup[0:NC, g, :, :].rearrange("p x d -> p (x d)"), B.ident[0:NC, 0:NC])
            last.then_inc(t_done, 1)

        @block.scalar
        def _(act):
            s_ = nc.scalar
            step = Chain(act, act_step)
            act.wait_ge(biased, 1)
            s_.activation(B.hbias[:], pbias[:], ACT.Copy)
            s_.activation(B.hbias_neg[:], pbias[:], ACT.Copy, scale=-1.0).then_inc(bias_ready, 1)
            act.wait_ge(bias_ready, 1)
            for c in range(2):
                act.wait_ge(hid_done, c + 1)
                s_.activation(first[64 * c:64 * c + 64, :], ph[0:64, c, 0:P], ACT.Copy)
                s_.activation(second[64 * c:64 * c + 64, :], ph[64:128, c, 0:P], ACT.Copy).then_inc(split, 1)
            act.wait_ge(summed_up, 1)
            s_.activation(gate[:], hid[:], ACT.Exp, bias=B.hbias_neg[:, 0:1], scale=-1.0).then_inc(exp_done, 1)
            act.wait_ge(ms_ready, 1)
            step(s_.activation(ms[0:NC, :], ms[0:NC, :], ACT.Ln, bias=B.eps[0:NC, 0:1], scale=1.0 / AD))
            s_.activation(ms[0:NC, :], ms[0:NC, :], ACT.Exp, scale=-0.5).then_inc(rstd_ready, 1)
            act.wait_ge(t_done, 1)
            s_.activation(B.kcT[:, :, 0:NC], pt[:, :, 0:NC], ACT.Copy)

        @block.vector
        def _(dve):
            v = nc.vector
            step = Chain(dve, dve_step)
            step(v.memset(B.vblk[:].rearrange("p g a d -> p (g a d)"), 0.0))
            dve.wait_ge(split, 2)
            v.tensor_tensor(hid[:], first[:, 0:4 * NC], second[:, 4:4 * NC + 4], ALU.add).then_inc(summed_up, 1)
            dve.wait_ge(exp_done, 1)
            step(v.tensor_scalar(gate[:], gate[:], 1.0, None, ALU.add))
            step(v.reciprocal(gate[:], gate[:]))
            v.scalar_tensor_tensor(hidg[:].rearrange("p g n -> p n g"), hid[:].rearrange("p (n g) -> p n g", g=KV), B.hbias[:, 0:1],
                                   gate[:].rearrange("p (n g) -> p n g", g=KV), ALU.add, ALU.mult).then_inc(hid_ready, 1)
            dve.wait_ge(kv_done, 1)
            for j in range(GRP):
                v.tensor_copy(B.vblk[32 * j:32 * j + NC, :, j, :], pv[32 * j:32 * j + NC, :].rearrange("p (g d) -> p g d", g=KV))
            kf = kdup[0:NC, :, 0, :]
            step(v.tensor_copy(kf, pk[0:NC, :].rearrange("p (g d) -> p g d", g=KV)))
            step(v.tensor_tensor(sq[0:NC], kf, kf, ALU.mult))
            v.tensor_reduce(ms[0:NC, :], sq[0:NC], AX, ALU.add).then_inc(ms_ready, 1)
            dve.wait_ge(rstd_ready, 1)
            step(v.tensor_tensor(kf, kf, ms[0:NC, :].unsqueeze(2).to_broadcast([NC, KV, AD]), ALU.mult))
            step(v.tensor_tensor(kf, kf, B.knw[0:NC, 0:AD].unsqueeze(1).to_broadcast([NC, KV, AD]), ALU.mult))
            v.tensor_copy(kdup[0:NC, :, 1, :], kf).then_inc(k_ready, 1)


def attend_prompt(nc, B, a, o):
    assert TP // BLK <= TOPN and TP <= WIN
    NC = NCMP_P
    with ExitStack() as ctx:
        sb = lambda n, s, d=F32: ctx.enter_context(nc.sbuf_tensor(n, s, d))
        ps = lambda n, s: ctx.enter_context(nc.psum_tensor(n, s, F32))
        qg, kg, vg = sb("a_q", [P, 2, TP]), sb("a_k", [P, 2, TP]), sb("a_v", [P, 2, 4, AD])
        kc, vb = sb("a_kc", [P, 32]), sb("a_vb", [P, GRP * AD])
        gg = sb("a_gates", [P, 4, 3, GRP])
        az = sb("a_siluz", [P, 4, GRP * AD])
        pc = sb("a_pc", [P, 4 * GRP, 32])
        pcT = sb("a_pcT", [P, 4, P])
        cmx, csum = sb("a_cmax", [P, 4 * GRP]), sb("a_csum", [P, 4 * GRP])
        acc = sb("a_acc", [P, 4, GRP * AD])
        prob, probT = sb("a_p", [P, 3, TP]), sb("a_pT", [P, 2, 4, P])
        nmx, rs, gr = sb("a_nmax", [P, 32]), sb("a_rowsum", [P, 32]), sb("a_gr", [P, 32])
        tmp = sb("a_tmp", [P, 2, GRP * AD])
        pS, pT, pO, pC = ps("a_pS", [P, 3, CH]), ps("a_pT2", [P, 2, CH]), ps("a_pO", [P, 2, CH]), ps("a_pC", [P, CH])
        with nc.Block() as block:
            @block.vector
            def _(dve):
                nc.vector.memset(pc[:].rearrange("p h n -> p (h n)"), 0.0)
        units = [(y, qt, h) for y in range(2) for qt in range(4) for h in range(GRP)]
        with nc.Fori(0, KV) as g, Semaphores(nc) as sem, ExitStack() as turn:
            staged, gates_ready, az_in = sem("a_staged"), sem("a_gates_ready"), sem("a_az_in")
            cs_done, cm_ready, c_exp, c_prob, ct_done, ct_ready, co_done, acc_ready = (sem(n) for n in (
                "a_cs", "a_cm", "a_cexp", "a_cprob", "a_ct", "a_ct_ready", "a_co", "a_acc_ready"))
            s_done, max_ready, p_ready, t_done, t_copied, o_done, o_used = (sem(n) for n in (
                "a_s", "a_max", "a_prob", "a_t", "a_tcopied", "a_o", "a_oused"))
            out_ready, stored, dve_step, act_step = sem("a_out"), sem("a_stored"), sem("a_dve"), sem("a_act")
            block = turn.enter_context(nc.Block())
            gi = bass.ds(g, 1)

            @block.sync
            def _(sp):
                cols = bass.ds(g * (GRP * AD), GRP * AD)
                sp.dma_start(az[:], B.gates_dram[2, 0:TP, cols].rearrange("(t p) n -> p t n", p=P)).then_inc(az_in, 16)
                SHARE = NPG // KV
                numbers = [sp.value_load(B.ptab[0:1, bass.ds(g * SHARE + i, 1)], min_val=0, max_val=a["pages"].shape[0] - 1)
                           for i in range(SHARE)]
                for i, page in enumerate(numbers):
                    sp.dma_start(B.comp[:, bass.ds(g * SHARE + i, 1), :].rearrange("p x c -> p (x c)"),
                                 a["pages"][bass.ds(page, 1), :, 0:CH].rearrange("x p c -> p (x c)")).then_inc(B.comp0_in, 16)
                seqs = bass.ds(g * (NB // KV), NB // KV)
                sp.dma_start(o["win_sample"][seqs, 0:WIN - TS, :], a["win_rows"][seqs, TS:WIN, :]).then_inc(B.win_kept, 16)
                out_cols = bass.ds(g * (GRP * AD) + MW, GRP * AD)
                for qt in range(4):
                    sp.wait_ge(out_ready, qt + 1)
                    sp.dma_start(B.cat_dram[qt * P:(qt + 1) * P, out_cols], acc[:, qt, :]).then_inc(stored, 16)
                sp.wait_ge(stored, 64)

            @block.gpsimd
            def _(pool):
                g_ = nc.gpsimd
                g_.tensor_copy(kc[:, 0:NC], B.kcT[:, gi, 0:NC].rearrange("p x n -> p (x n)"))
                g_.tensor_copy(vb[:], B.vblk[:, gi, :, :].rearrange("p x a d -> p (x a d)"))
                g_.tensor_copy(vg[:, 0], B.vsel[:, :, bass.ds(g * AD, AD)])
                g_.tensor_copy(vg[:, 1], B.vwin[:, :, bass.ds(g * AD, AD)]).then_inc(staged, 1)
                g_.tensor_copy(gg[:], B.gsig[:, 0:4, :].rearrange("p t (y h) -> p t y h", y=3)[:, :, :, bass.ds(g * GRP, GRP)])\
                    .then_inc(gates_ready, 1)

            @block.tensor
            def _(pe):
                pe.wait_ge(staged, 3)
                for par, bank in enumerate((pC[:], pS[:, 2, :])):
                    half = slice(64 * par, 64 * par + 64)
                    for qt in range(4):
                        for h2 in range(2):
                            last = nc.tensor.matmul(bank[:, (qt * 2 + h2) * 32:(qt * 2 + h2) * 32 + NC], qg[half, h2, qt * P:(qt + 1) * P],
                                                    kc[half, 0:NC], start=True, stop=True)
                last.then_inc(cs_done, 1)

                def scores(u):
                    y, qt, h = units[u]
                    half = slice(64 * (h % 2), 64 * (h % 2) + 64)
                    if u == 2:
                        pe.wait_ge(cm_ready, 1)
                    if u >= 3:
                        pe.wait_ge(p_ready, u - 2)
                    nc.tensor.matmul(pS[:, u % 3, 0:(qt + 1) * P], qg[half, h // 2, qt * P:(qt + 1) * P],
                                     kg[half, y, 0:(qt + 1) * P], start=True, stop=True).then_inc(s_done, 1)

                def turned(u):
                    y, qt, h = units[u]
                    pe.wait_ge(p_ready, u + 1)
                    if u >= 2:
                        pe.wait_ge(t_copied, u - 1)
                    elif u == 0:
                        pe.wait_ge(ct_ready, 1)
                    for i in range(qt + 1):
                        last = nc.tensor.transpose(pT[:, u % 2, i * P:(i + 1) * P], prob[:, u % 3, i * P:(i + 1) * P], B.ident[:])
                    last.then_inc(t_done, 1)

                def values(u):
                    y, qt, h = units[u]
                    r = u // GRP
                    pe.wait_ge(t_copied, u + 1)
                    if h == 0:
                        if r >= 2:
                            pe.wait_ge(o_used, r - 1)
                        else:
                            pe.wait_ge(acc_ready, 1)
                    for i in range(qt + 1):
                        last = nc.tensor.matmul(pO[:, r % 2, h * AD:(h + 1) * AD], probT[:, u % 2, i, :], vg[:, y, i, :],
                                                start=i == 0, stop=i == qt)
                    last.then_inc(o_done, 1)

                scores(0)
                scores(1)
                pe.wait_ge(c_prob, 1)
                for qt in range(4):
                    last = nc.tensor.transpose(pT[:, 0, qt * P:(qt + 1) * P],
                                               pc[:, qt * GRP:(qt + 1) * GRP, :].rearrange("p h n -> p (h n)"), B.ident[:])
                last.then_inc(ct_done, 1)
                pe.wait_ge(ct_ready, 1)
                for qt in range(4):
                    last = nc.tensor.matmul(pO[:, qt // 2, (qt % 2) * 256:(qt % 2 + 1) * 256], pcT[:, qt, :], vb[:], start=True, stop=True)
                last.then_inc(co_done, 1)
                n = len(units)
                for u in range(n + 2):
                    if u + 2 < n:
                        scores(u + 2)
                    if u < n:
                        turned(u)
                    if u >= 1 and u - 1 < n:
                        values(u - 1)

            @block.scalar
            def _(act):
                s_ = nc.scalar
                s_.activation(qg[:], B.qT[:, bass.ds(g * 2, 2), :], ACT.Copy).then_inc(staged, 1)
                act.wait_ge(cm_ready, 1)
                s_.activation(pc[:, :, 0:NC], pc[:, :, 0:NC], ACT.Exp).then_inc(c_exp, 1)
                act.wait_ge(ct_done, 1)
                s_.activation(pcT[:].rearrange("p t q -> p (t q)"), pT[:, 0, :], ACT.Copy).then_inc(ct_ready, 1)
                n = len(units)

                def copied(u):
                    y, qt, h = units[u]
                    act.wait_ge(t_done, u + 1)
                    if u >= 2:
                        act.wait_ge(o_done, u - 1)
                    s_.activation(probT[:, u % 2, 0:qt + 1, :], pT[:, u % 2, 0:(qt + 1) * P].rearrange("p (t q) -> p t q", q=P),
                                  ACT.Copy).then_inc(t_copied, 1)

                for u in range(n):
                    y, qt, h = units[u]
                    act.wait_ge(max_ready, u + 1)
                    if u >= 3:
                        act.wait_ge(t_done, u - 2)
                    s_.activation(prob[:, u % 3, 0:(qt + 1) * P], pS[:, u % 3, 0:(qt + 1) * P], ACT.Exp, bias=nmx[:, u:u + 1],
                                  accum_out=rs[:, u:u + 1]).then_inc(p_ready, 1)
                    if u >= 1:
                        copied(u - 1)
                copied(n - 1)

            @block.vector
            def _(dve):
                v = nc.vector
                step = Chain(dve, dve_step)
                v.tensor_copy(kg[:, 0, :], B.ksel[:, gi, :].rearrange("p x t -> p (x t)"))
                v.tensor_copy(kg[:, 1, :], B.kwin[:, gi, :].rearrange("p x t -> p (x t)")).then_inc(staged, 1)
                dve.wait_ge(cs_done, 1)
                cp = pc[:, :, 0:NC]
                for par, bank in enumerate((pC[:], pS[:, 2, :])):
                    last = v.tensor_tensor(pc[:].rearrange("p (t h x) n -> p x t h n", h=2, x=2)[:, par, :, :, 0:NC],
                                           bank[:, 0:256].rearrange("p (t h n) -> p t h n", t=4, h=2)[:, :, :, 0:NC],
                                           B.cmpmask[:, :, 0:NC].unsqueeze(2).to_broadcast([P, 4, 2, NC]), ALU.add)
                step(last)
                step(v.tensor_reduce(cmx[:], cp, AX, ALU.max))
                step(v.tensor_scalar(cmx[:], cmx[:], -1e20, None, ALU.max))
                v.tensor_tensor(cp, cp, cmx[:].unsqueeze(2).to_broadcast([P, 4 * GRP, NC]), ALU.subtract).then_inc(cm_ready, 1)

                def maximum(u):
                    y, qt, h = units[u]
                    dve.wait_ge(s_done, u + 1)
                    diag = pS[:, u % 3, qt * P:(qt + 1) * P]
                    step(v.tensor_tensor(diag, diag, B.causal[:], ALU.add))
                    v.tensor_reduce(nmx[:, u:u + 1], pS[:, u % 3, 0:(qt + 1) * P], AX, ALU.max, negate=True).then_inc(max_ready, 1)

                dve.wait_ge(c_exp, 1)
                step(v.tensor_reduce(csum[:], cp, AX, ALU.add))
                step(v.tensor_scalar(csum[:], csum[:], 1e-30, None, ALU.max))
                step(v.reciprocal(csum[:], csum[:]))
                v.tensor_tensor(cp, cp, csum[:].unsqueeze(2).to_broadcast([P, 4 * GRP, NC]), ALU.mult).then_inc(c_prob, 1)
                maximum(0)
                maximum(1)
                dve.wait_ge(gates_ready, 1)
                dve.wait_ge(co_done, 1)
                for qt in range(4):
                    last = v.tensor_tensor(acc[:, qt, :].rearrange("p (h d) -> p h d", d=AD),
                                           pO[:, qt // 2, (qt % 2) * 256:(qt % 2 + 1) * 256].rearrange("p (h d) -> p h d", d=AD),
                                           gg[:, qt, 0, :].unsqueeze(2).to_broadcast([P, GRP, AD]), ALU.mult)
                last.then_inc(acc_ready, 1)
                dve.wait_ge(acc_ready, 1)

                def gather(r):
                    y, qt, _h = units[r * GRP]
                    dve.wait_ge(o_done, (r + 1) * GRP)
                    us = slice(r * GRP, (r + 1) * GRP)
                    step(v.reciprocal(gr[:, us], rs[:, us]))
                    step(v.tensor_tensor(gr[:, us], gr[:, us], gg[:, qt, 1 + y, :], ALU.mult))
                    v.tensor_tensor(tmp[:, r % 2, :].rearrange("p (h d) -> p h d", d=AD),
                                    pO[:, r % 2, 0:256].rearrange("p (h d) -> p h d", d=AD),
                                    gr[:, us].unsqueeze(2).to_broadcast([P, GRP, AD]), ALU.mult).then_inc(o_used, 1)
                    dve.wait_ge(o_used, r + 1)
                    step(v.tensor_tensor(acc[:, qt, :], acc[:, qt, :], tmp[:, r % 2, :], ALU.add))
                    if y == 1:
                        dve.wait_ge(az_in, 16)
                        v.tensor_tensor(acc[:, qt, :], acc[:, qt, :], az[:, qt, :], ALU.mult).then_inc(out_ready, 1)

                n = len(units)
                for u in range(2, n):
                    maximum(u)
                    if u % GRP == 1 and u > GRP:
                        gather(u // GRP - 1)
                gather(n // GRP - 1)


def attend_samples(nc, B, a, o):
    with ExitStack() as ctx:
        sb = lambda n, s, d=F32: ctx.enter_context(nc.sbuf_tensor(n, s, d))
        ps = lambda n, s: ctx.enter_context(nc.psum_tensor(n, s, F32))
        S = B.sample = Buffers()
        S.comp, S.kvp = B.comp, sb("s_kv", [P, NPG, CH])
        S.wnd = sb("s_wnd", [P, 2 * 2 * WIN])
        S.cw1 = sb("cw1_sample", [P, 2, 8, P])
        S.scores = sb("s_scores", [P, PAST + TSA])
        S.first, S.second = sb("s_first", [P, KV * PAST // SEG]), sb("s_second", [P, KV * PAST // SEG])
        S.hidg = sb("s_hidg", [P, KV, NCMP_S + 1])
        S.kcn, S.kcms = sb("s_kcn", [P, 2, KV * AD]), sb("s_kcms", [P, 2 * KV])
        S.kcT, S.vc = sb("s_kcT", [P, 2, 256]), sb("s_vc", [P, 2, KV * AD])
        S.probT = sb("s_probT", [P, 2, 4, P])
        S.qb, S.nm = sb("s_qb", [P, 2, 64]), sb("s_newmask", [P, TSA])
        S.pgp, S.imp, S.top = sb("s_pgp", [32, 264]), sb("s_imp", [32, 72]), sb("s_top", [32, 2, 8])
        S.bias = sb("s_bias", [P, NBLK])
        S.mx, S.rs, S.col = sb("s_mx", [P, 16]), sb("s_rs", [P, 16]), sb("s_col", [P, 8])
        S.rows = sb("s_rows", [P, 3, AD])
        S.pS, S.pT, S.pO, S.pH = (ps(n, [P, 2, CH]) for n in ("s_pS", "s_pT", "s_pO", "s_pH"))
        with Semaphores(nc) as sem, nc.Block() as block:
            loaded, zero = sem("s_loaded"), sem("s_zero")

            @block.sync
            def _(sp):
                sp.dma_start(S.cw1[:], a["cmp_w1"]).then_inc(loaded, 16)
                sp.wait_ge(loaded, 16)
                sp.wait_ge(B.comp0_in, 16 * NPG)

            @block.vector
            def _(dve):
                nc.vector.memset(S.imp[:], 0.0)
                nc.vector.memset(S.kcn[:], 0.0)
                nc.vector.memset(S.pgp[:], 0.0).then_inc(zero, 1)
                dve.wait_ge(zero, 1)
        sample_turn(nc, B, a, -1, attend=False, compress=True, load=True)
        with nc.Fori(0, NB - 2) as b:
            sample_turn(nc, B, a, b, attend=True, compress=True, load=True)
        sample_turn(nc, B, a, NB - 2, attend=True, compress=True, load=False)
        sample_turn(nc, B, a, NB - 1, attend=True, compress=False, load=False)


def load_pages(sp, ptab, pages, dst, part, first, begin, end, sem):
    AHEAD = 8
    assert begin % AHEAD == 0 and end % AHEAD == 0
    with sp.Fori(begin // AHEAD, end // AHEAD) as i:
        numbers = [sp.value_load(ptab[0:1, bass.ds(first + i * AHEAD + j, 1)], min_val=0, max_val=pages.shape[0] - 1)
                   for j in range(AHEAD)]
        for j, page in enumerate(numbers):
            sp.dma_start(dst[:, bass.ds(i * AHEAD + j, 1), :].rearrange("p x c -> p (x c)"),
                         pages[bass.ds(page, 1), :, part * CH:(part + 1) * CH].rearrange("x p c -> p (x c)")).then_inc(sem, 16)


def sample_turn(nc, B, a, b, attend, compress, load):
    S = B.sample
    NC = NCMP_S
    NQ = PAST // CH
    PQ = NPG // 4
    SC = S.scores
    pw, pc = SC[:, 0:WIN + TSA], SC[:, 1024:1024 + NC]
    pcT = SC[:, 1280:1536].rearrange("p (n r) -> p n r", r=P)
    pwT = SC[:, 2048:2048 + 5 * P].rearrange("p (n r) -> p n r", r=P)
    SN = SC[:, PAST:PAST + TSA]
    NH = KV * NC
    gate, csq = S.second[:, 0:NH], S.second[:, 0:2 * KV * AD]
    with Semaphores(nc) as sem, ExitStack() as turn:
        kv_in = [sem(f"s_kv_in{i}") for i in range(4)]
        wnd_in, comp_in, stored, staged = (sem(n) for n in ("s_wnd_in", "s_comp_in", "s_stored", "s_staged"))
        cs_done, ws_done, cm_ready, wm_ready, c_exp, c_prob, w_prob = (sem(n) for n in (
            "s_cs", "s_ws", "s_cm", "s_wm", "s_cexp", "s_cprob", "s_wprob"))
        ct_done, ct_ready, co_done = (sem(n) for n in ("s_ct", "s_ctr", "s_co"))
        wt_done, wt_ready, wo_done = (sem(n) for n in ("s_wt", "s_wtr", "s_wo"))
        pg_read, sel_mask, bias_done, bias_read = (sem(n) for n in ("s_pg", "s_selmask", "s_bias_done", "s_bias_read"))
        ss_done, sc_evac, mx_ready, p_ready, t_done, t_copied, pv_done = (sem(n) for n in (
            "s_ss", "s_sce", "s_mxr", "s_p", "s_t", "s_tc", "s_pv"))
        rows_ready = sem("s_rowsr")
        h_done, h_split, hid_sum, sig_ready, hid_ready, kv_done, kc_copied, ms_ready, rstd_ready, kcn_ready, kt_done = (
            sem(n) for n in ("s_h", "s_hsplit", "s_hsum", "s_sig", "s_hid", "s_kvd", "s_kcc", "s_ms", "s_rstd", "s_kcnr", "s_kt"))
        act_step, dve_step, pool_step = sem("s_act_step"), sem("s_dve_step"), sem("s_pool_step")
        block = turn.enter_context(nc.Block())

        @block.sync
        def _(sp):
            if attend:
                sp.dma_start(S.wnd[:], a["win_pages"][bass.ds(b, 1)].rearrange("x p c -> p (x c)")).then_inc(wnd_in, 16)
                for q in range(3):
                    load_pages(sp, B.ptab, a["pages"], S.kvp, 1, b * NPG, q * PQ, (q + 1) * PQ, kv_in[q])
            if load:
                for half in range(2):
                    sp.wait_ge(h_done, 2 * half + 2)
                    load_pages(sp, B.ptab, a["pages"], S.comp, 0, (b + 2) * NPG, half * NPG // 2, (half + 1) * NPG // 2, comp_in)
                sp.wait_ge(comp_in, 16 * NPG)
            if attend:
                for q in range(4):
                    sp.wait_ge(kv_in[q], 16 * PQ)
                sp.wait_ge(rows_ready, 3)
                for y, kind in enumerate((0, 2, 1)):
                    sp.dma_start(B.o_dram[kind, bass.ds(b, 1)].rearrange("x t (h d) -> (x h) t d", d=AD), S.rows[:, y, :]).then_inc(stored, 16)
                sp.wait_ge(stored, 48)

        @block.tensor
        def _(pe):
            mm, tp = nc.tensor.matmul, nc.tensor.transpose

            def hidden(i):
                if not compress:
                    return
                cc, c = i // 2, i % 2
                if i >= 2:
                    pe.wait_ge(h_split, i - 1)
                for k in range(8):
                    last = mm(S.pH[:, c, :], S.cw1[:, c, k, :], S.comp[:, 16 * cc:16 * cc + 16, k * 64 + c * 32:k * 64 + c * 32 + 32],
                              start=k == 0, stop=k == 7)
                last.then_inc(h_done, 1)

            def second_layer():
                pe.wait_ge(hid_ready, 1)
                for c in range(2):
                    half = slice(64 * c, 64 * c + 64)
                    for nt in range(2):
                        n = min(P, NC - nt * P)
                        for g in range(KV):
                            last = mm(S.pH[0:n, c, nt * 256 + g * AD:nt * 256 + (g + 1) * AD], S.hidg[half, g, nt * P:nt * P + n],
                                      B.cw2[half, :], start=True, stop=True)
                last.then_inc(kv_done, 1)

            def keys_turned():
                pe.wait_ge(kcn_ready, 1)
                for gp in range(2):
                    for nt in range(2):
                        n = min(P, NC - nt * P)
                        last = tp(S.pH[:, 0, gp * 256 + nt * P:gp * 256 + nt * P + n], S.kcn[0:n, nt, gp * P:(gp + 1) * P],
                                  B.ident[0:n, 0:n])
                last.then_inc(kt_done, 1)

            if not attend:
                for i in range(4):
                    hidden(i)
                second_layer()
                keys_turned()
                return
            pe.wait_ge(staged, 1)
            for gp in range(2):
                mm(S.pS[64 * gp:64 * gp + 64, 0, 0:NC], S.qb[:, gp, :], S.kcT[:, gp, 0:NC], start=True, stop=True)
                last = mm(S.pS[64 * gp:64 * gp + 64, 0, 256:256 + TSA], S.qb[:, gp, :], B.kwin_new[:, gp, :], start=True, stop=True)
            last.then_inc(cs_done, 1)
            hidden(0)
            pe.wait_ge(wnd_in, 16)
            for gp in range(2):
                last = mm(S.pS[64 * gp:64 * gp + 64, 1, :], S.qb[:, gp, :], S.wnd[:, gp * WIN:(gp + 1) * WIN], start=True, stop=True)
            last.then_inc(ws_done, 1)
            pe.wait_ge(c_prob, 1)
            for nt in range(2):
                n = min(P, NC - nt * P)
                tp(S.pT[0:n, 0, nt * P:(nt + 1) * P], pc[:, nt * P:nt * P + n], B.ident[:])
            mm(S.pT[0:32, 1, 0:NC], B.fold[:], pc, start=True, stop=True).then_inc(ct_done, 1)
            hidden(1)
            pe.wait_ge(ct_ready, 1)
            for nt in range(2):
                n = min(P, NC - nt * P)
                last = mm(S.pO[:, 0, 0:256], pcT[0:n, nt, :], S.vc[0:n, nt, :], start=nt == 0, stop=nt == 1)
            last.then_inc(co_done, 1)
            pe.wait_ge(w_prob, 1)
            pe.wait_ge(pg_read, 1)
            for i in range(4):
                tp(S.pT[:, 0, i * P:(i + 1) * P], pw[:, i * P:(i + 1) * P], B.ident[:])
            tp(S.pT[0:TSA, 1, 256:256 + P], pw[:, WIN:WIN + TSA], B.ident[:]).then_inc(wt_done, 1)
            hidden(2)
            pe.wait_ge(wt_ready, 1)
            for i in range(4):
                mm(S.pO[:, 1, 0:256], pwT[:, i, :], S.wnd[:, 2 * WIN + i * 256:2 * WIN + (i + 1) * 256], start=i == 0, stop=False)
            last = mm(S.pO[:, 1, 0:256], pwT[0:TSA, 4, :], B.vwin_new[:], start=False, stop=True)
            last.then_inc(wo_done, 1)
            pe.wait_ge(sel_mask, 1)
            mm(S.pT[:, 1, 0:NBLK], B.unfold[:], S.imp[:, 0:NBLK], start=True, stop=True).then_inc(bias_done, 1)
            hidden(3)
            for j in range(NQ + 1):
                if j < NQ and j % 2 == 0:
                    pe.wait_ge(kv_in[j // 2], 16 * PQ)
                if j >= 2:
                    pe.wait_ge(sc_evac, j - 1)
                for gp in range(2):
                    if j < NQ:
                        last = mm(S.pS[64 * gp:64 * gp + 64, j % 2, :], S.qb[:, gp, :], S.kvp[:, 4 * j:4 * j + 4, gp * P:(gp + 1) * P],
                                  start=True, stop=True)
                    else:
                        last = mm(S.pS[64 * gp:64 * gp + 64, j % 2, 0:TSA], S.qb[:, gp, :], B.ksel_new[:, gp, :], start=True, stop=True)
                last.then_inc(ss_done, 1)
            pe.wait_ge(bias_read, 1)
            pe.wait_ge(rows_ready, 2)
            for j in range(NQ + 2):
                if j <= NQ:
                    pe.wait_ge(p_ready, j + 1)
                    if j >= 2:
                        pe.wait_ge(t_copied, j - 1)
                    if j < NQ:
                        for i in range(4):
                            last = tp(S.pT[:, j % 2, i * P:(i + 1) * P], SC[:, j * CH + i * P:j * CH + (i + 1) * P], B.ident[:])
                    else:
                        last = tp(S.pT[0:TSA, j % 2, 0:P], SN, B.ident[:])
                    last.then_inc(t_done, 1)
                if j >= 1:
                    q = j - 1
                    pe.wait_ge(t_copied, q + 1)
                    for i in range(4 if q < NQ else 1):
                        if q < NQ:
                            last = mm(S.pO[:, 0, 0:256], S.probT[:, q % 2, i, :], S.kvp[:, 4 * q + i, 256:512], start=q == 0 and i == 0, stop=False)
                        else:
                            last = mm(S.pO[:, 0, 0:256], S.probT[0:TSA, q % 2, 0, :], B.vsel_new[:], start=False, stop=True)
                    last.then_inc(pv_done, 1)
                if j == 2 and compress:
                    second_layer()
            if compress:
                keys_turned()

        @block.scalar
        def _(act):
            s_ = nc.scalar
            step = Chain(act, act_step)

            def split(i):
                if not compress:
                    return
                cc, c = i // 2, i % 2
                act.wait_ge(h_done, i + 1)
                s_.activation(S.first[64 * c:64 * c + 64, cc * CH:(cc + 1) * CH], S.pH[0:64, c, :], ACT.Copy)
                s_.activation(S.second[64 * c:64 * c + 64, cc * CH:(cc + 1) * CH], S.pH[64:128, c, :], ACT.Copy).then_inc(h_split, 1)

            def silu():
                act.wait_ge(hid_sum, 1)
                step(s_.activation(gate, S.first[:, 0:NH], ACT.Exp, bias=B.hbias_neg[:, 0:1], scale=-1.0))
                step(s_.activation(gate, gate, ACT.Ln, bias=1.0))
                s_.activation(gate, gate, ACT.Exp, scale=-1.0).then_inc(sig_ready, 1)

            def second_layer():
                act.wait_ge(kv_done, 1)
                if attend:
                    act.wait_ge(co_done, 1)
                for nt in range(2):
                    n = min(P, NC - nt * P)
                    s_.activation(S.vc[0:n, nt, :], S.pH[0:n, 1, nt * 256:(nt + 1) * 256], ACT.Copy)
                for nt in range(2):
                    n = min(P, NC - nt * P)
                    last = s_.activation(S.kcn[0:n, nt, :], S.pH[0:n, 0, nt * 256:(nt + 1) * 256], ACT.Copy)
                last.then_inc(kc_copied, 1)

            def norm():
                act.wait_ge(ms_ready, 1)
                step(s_.activation(S.kcms[:], S.kcms[:], ACT.Ln, bias=B.eps[:, 0:1], scale=1.0 / AD))
                s_.activation(S.kcms[:], S.kcms[:], ACT.Exp, scale=-0.5).then_inc(rstd_ready, 1)

            def keys_turned():
                act.wait_ge(kt_done, 1)
                s_.activation(S.kcT[:, :, 0:NC], S.pH[:, 0, :].rearrange("p (g n) -> p g n", g=2)[:, :, 0:NC], ACT.Copy)

            if not attend:
                for i in range(4):
                    split(i)
                silu()
                second_layer()
                norm()
                keys_turned()
                return
            s_.activation(S.qb[:], B.qblk[:, :, bass.ds(b, 1), :].rearrange("p g x c -> p g (x c)"), ACT.Copy).then_inc(staged, 1)
            load_pages(act, B.ptab, a["pages"], S.kvp, 1, b * NPG, 3 * PQ, NPG, kv_in[3])
            act.wait_ge(cm_ready, 1)
            s_.activation(pc, S.pS[:, 0, 0:NC], ACT.Exp, bias=S.mx[:, 12:13], accum_out=S.rs[:, 12:13]).then_inc(c_exp, 1)
            act.wait_ge(wm_ready, 1)
            s_.activation(pw[:, 0:WIN], S.pS[:, 1, :], ACT.Exp, bias=S.mx[:, 13:14], accum_out=S.rs[:, 13:14])
            s_.activation(pw[:, WIN:WIN + TSA], S.pS[:, 0, 256:256 + TSA], ACT.Exp, bias=S.mx[:, 13:14],
                          accum_out=S.rs[:, 14:15]).then_inc(w_prob, 1)
            split(0)
            act.wait_ge(ct_done, 1)
            for nt in range(2):
                n = min(P, NC - nt * P)
                last = s_.activation(pcT[0:n, nt, :], S.pT[0:n, 0, nt * P:(nt + 1) * P], ACT.Copy)
            last.then_inc(ct_ready, 1)
            act.wait_ge(wt_done, 1)
            s_.activation(pwT[:, 0:4, :], S.pT[:, 0, :].rearrange("p (n r) -> p n r", r=P), ACT.Copy)
            s_.activation(pwT[0:TSA, 4, :], S.pT[0:TSA, 1, 256:256 + P], ACT.Copy).then_inc(wt_ready, 1)
            split(1)
            split(2)
            split(3)
            if compress:
                silu()
            act.wait_ge(mx_ready, 1)
            for j in range(NQ + 1):
                src = SC[:, j * CH:(j + 1) * CH] if j < NQ else SN
                s_.activation(src, src, ACT.Exp, bias=S.mx[:, 11:12], accum_out=S.rs[:, j:j + 1]).then_inc(p_ready, 1)
            if compress:
                second_layer()
                norm()
            if compress:
                keys_turned()

        @block.vector
        def _(dve):
            if not attend:
                return
            v = nc.vector
            step = Chain(dve, dve_step)
            own = lambda bank, g: bank[32 * g:32 * g + 32, g * AD:(g + 1) * AD]
            step(v.tensor_copy(S.nm[:], B.newmask[:, bass.ds(b * TSA, TSA)]))
            dve.wait_ge(cs_done, 1)
            v.tensor_reduce(S.mx[:, 12:13], S.pS[:, 0, 0:NC], AX, ALU.max, negate=True).then_inc(cm_ready, 1)
            wnew = S.pS[:, 0, 256:256 + TSA]
            dve.wait_ge(c_exp, 1)
            step(v.reciprocal(S.rs[:, 12:13], S.rs[:, 12:13]))
            v.tensor_scalar(pc, pc, S.rs[:, 12:13], None, ALU.mult).then_inc(c_prob, 1)
            v.tensor_tensor(wnew, wnew, S.nm[:], ALU.add)
            dve.wait_ge(ws_done, 1)
            step(v.tensor_tensor(S.pS[:, 1, 0:TS], S.pS[:, 1, 0:TS], B.winmask[:], ALU.add))
            v.tensor_reduce(S.mx[:, 13:14], wnew, AX, ALU.max, negate=True)
            step(v.tensor_reduce(S.mx[:, 14:15], S.pS[:, 1, :], AX, ALU.max, negate=True))
            v.tensor_tensor(S.mx[:, 13:14], S.mx[:, 13:14], S.mx[:, 14:15], ALU.min).then_inc(wm_ready, 1)
            dve.wait_ge(w_prob, 1)
            step(v.tensor_tensor(S.col[:, 0:1], S.rs[:, 13:14], S.rs[:, 14:15], ALU.add))
            step(v.reciprocal(S.col[:, 0:1], S.col[:, 0:1]))
            dve.wait_ge(ct_done, 1)
            v.tensor_copy(S.pgp[:, 1:1 + NC], S.pT[0:32, 1, 0:NC]).then_inc(pg_read, 1)
            dve.wait_ge(pg_read, 1)
            imp = S.imp[:, 0:NBLK]
            step(v.tensor_reduce(imp, S.pgp[:, 0:4 * NBLK].rearrange("p (k r) -> p k r", r=4), AX, ALU.add))
            step(v.tensor_tensor(imp, imp, S.pgp[:, 4:4 + 4 * NBLK].rearrange("p (k r) -> p k r", r=4)[:, :, 0], ALU.add))
            v.memset(S.imp[:, 0:1], -NEG)
            step(v.memset(S.imp[:, NBLK - 2:NBLK], -NEG))
            for r in range(TOPN // 8):
                step(v.max(S.top[:, r, :], imp))
                step(v.match_replace(imp, S.top[:, r, :], imp, NEG))
            v.tensor_scalar(imp, imp, NEG / 10, None, ALU.is_gt).then_inc(sel_mask, 1)
            dve.wait_ge(bias_done, 1)
            v.tensor_scalar(S.bias[:], S.pT[:, 1, 0:NBLK], NEG, None, ALU.mult).then_inc(bias_read, 1)
            dve.wait_ge(bias_read, 1)
            dve.wait_ge(co_done, 1)
            for g in range(KV):
                last = v.tensor_copy(S.rows[32 * g:32 * g + 32, 0, :], own(S.pO[:, 0, :], g))
            last.then_inc(rows_ready, 1)
            for j in range(NQ + 1):
                dve.wait_ge(ss_done, j + 1)
                if j < NQ:
                    dst = SC[:, j * CH:(j + 1) * CH]
                    last = v.tensor_tensor(dst.rearrange("p (k x) -> p k x", x=BLK), S.pS[:, j % 2, :].rearrange("p (k x) -> p k x", x=BLK),
                                           S.bias[:, 8 * j:8 * j + 8].unsqueeze(2).to_broadcast([P, 8, BLK]), ALU.add)
                else:
                    dst = SN
                    last = v.tensor_tensor(dst, S.pS[:, j % 2, 0:TSA], S.nm[:], ALU.add)
                last.then_inc(sc_evac, 1)
                dve.wait_ge(sc_evac, j + 1)
                last = v.tensor_reduce(S.mx[:, j:j + 1], dst, AX, ALU.max)
            step(last)
            v.tensor_reduce(S.mx[:, 11:12], S.mx[:, 0:NQ + 1], AX, ALU.max, negate=True).then_inc(mx_ready, 1)
            dve.wait_ge(wo_done, 1)
            for g in range(KV):
                rows = slice(32 * g, 32 * g + 32)
                last = v.tensor_scalar(S.rows[rows, 1, :], own(S.pO[:, 1, :], g), S.col[rows, 0:1], None, ALU.mult)
            last.then_inc(rows_ready, 1)
            for j in range(NQ + 1):
                dve.wait_ge(t_done, j + 1)
                if j >= 2:
                    dve.wait_ge(pv_done, j - 1)
                if j < NQ:
                    last = v.tensor_copy(S.probT[:, j % 2], S.pT[:, j % 2, :].rearrange("p (n r) -> p n r", r=P))
                else:
                    last = v.tensor_copy(S.probT[0:TSA, j % 2, 0, :], S.pT[0:TSA, j % 2, 0:P])
                last.then_inc(t_copied, 1)
            step(v.tensor_reduce(S.col[:, 1:2], S.rs[:, 0:NQ + 1], AX, ALU.add))
            step(v.reciprocal(S.col[:, 1:2], S.col[:, 1:2]))
            dve.wait_ge(pv_done, NQ + 1)
            for g in range(KV):
                rows = slice(32 * g, 32 * g + 32)
                last = v.tensor_scalar(S.rows[rows, 2, :], own(S.pO[:, 0, :], g), S.col[rows, 1:2], None, ALU.mult)
            last.then_inc(rows_ready, 1)

        @block.gpsimd
        def _(pool):
            g_ = nc.gpsimd
            step = Chain(pool, pool_step)
            if compress:
                pool.wait_ge(h_split, 4)
                g_.tensor_tensor(S.first[:, 0:NH], S.first[:, 0:NH], S.second[:, KV:NH + KV], ALU.add).then_inc(hid_sum, 1)
                pool.wait_ge(sig_ready, 1)
                step(g_.tensor_scalar(S.first[:, 0:NH], S.first[:, 0:NH], B.hbias[:, 0:1], None, ALU.add))
                g_.tensor_tensor(S.hidg[:, :, 0:NC].rearrange("p g n -> p n g"), S.first[:, 0:NH].rearrange("p (n g) -> p n g", g=KV),
                                 gate.rearrange("p (n g) -> p n g", g=KV), ALU.mult).then_inc(hid_ready, 1)
                pool.wait_ge(kc_copied, 1)
                kf = S.kcn[:].rearrange("p n c -> p (n c)")
                k3 = S.kcn[:].rearrange("p n (g d) -> p (n g) d", d=AD)
                step(g_.tensor_tensor(csq, kf, kf, ALU.mult))
                w = AD
                c3 = csq.rearrange("p (x d) -> p x d", d=AD)
                while w > 2:
                    w //= 2
                    step(g_.tensor_tensor(c3[:, :, 0:w], c3[:, :, 0:w], c3[:, :, w:2 * w], ALU.add))
                g_.tensor_tensor(S.kcms[:].unsqueeze(2), c3[:, :, 0:1], c3[:, :, 1:2], ALU.add).then_inc(ms_ready, 1)
                pool.wait_ge(rstd_ready, 1)
                step(g_.tensor_tensor(k3, k3, S.kcms[:].unsqueeze(2).to_broadcast([P, 2 * KV, AD]), ALU.mult))
                g_.tensor_tensor(k3, k3, B.knw[:, 0:AD].unsqueeze(1).to_broadcast([P, 2 * KV, AD]), ALU.mult).then_inc(kcn_ready, 1)


def combine_samples(nc, B, a, o):
    with Semaphores(nc) as sem, ExitStack() as ctx:
        sb = lambda n, s, d=F32: ctx.enter_context(nc.sbuf_tensor(n, s, d))
        rows, az = sb("cb_rows", [TSA, 3, AW]), sb("cb_az", [TSA, AW])
        loaded, az_in, done, stored, dve_step = (sem(n) for n in ("cb_in", "cb_az_in", "cb_done", "cb_stored", "cb_dve"))
        block = ctx.enter_context(nc.Block())

        @block.sync
        def _(sp):
            sp.dma_start(rows[:], B.o_dram.rearrange("y b t c -> (b t) y c")).then_inc(loaded, 16)
            sp.dma_start(az[:], B.gates_dram[2, TP:T, :]).then_inc(az_in, 16)
            sp.wait_ge(done, 1)
            sp.dma_start(B.cat_dram[TP:T, MW:D], rows[:, 0, :]).then_inc(stored, 16)
            sp.wait_ge(stored, 16)

        @block.scalar
        def _(act):
            act.wait_ge(B.win_kept, 16 * KV)

        @block.vector
        def _(dve):
            v = nc.vector
            step = Chain(dve, dve_step)
            dve.wait_ge(loaded, 16)
            for y in range(3):
                r = rows[:, y, :].rearrange("p (h d) -> p h d", d=AD)
                last = v.tensor_tensor(r, r, B.gsig[0:TSA, 4, y * AH:(y + 1) * AH].unsqueeze(2).to_broadcast([TSA, AH, AD]), ALU.mult)
            step(last)
            step(v.tensor_tensor(rows[:, 0, :], rows[:, 0, :], rows[:, 1, :], ALU.add))
            step(v.tensor_tensor(rows[:, 0, :], rows[:, 0, :], rows[:, 2, :], ALU.add))
            dve.wait_ge(az_in, 16)
            v.tensor_tensor(rows[:, 0, :], rows[:, 0, :], az[:], ALU.mult).then_inc(done, 1)


def project_out(nc, B, a, o):
    NT, HALF, WCH = len(TILES), T // 2, 2 * P
    NC = D // WCH
    GT = KD // 4
    NG = GT * NT
    halves = [slice(0, HALF), slice(HALF, T)]
    with Semaphores(nc) as sem, ExitStack() as ctx:
        sb = lambda n, s, d=F32: ctx.enter_context(nc.sbuf_tensor(n, s, d))
        ps = lambda n, s: ctx.enter_context(nc.psum_tensor(n, s, F32))
        fhi, flo = sb("o_feat_hi", [P, KD, T], F32R), sb("o_feat_lo", [P, KD, T], F32R)
        h = sb("o_h", [P, KD, T])
        raw = sb("o_w_raw", [P, 2, KD, WCH])
        whi, wlo = sb("o_w_hi", [P, 2, KD, P], F32R), sb("o_w_lo", [P, 2, KD, P], F32R)
        proj, pfm = sb("o_proj", [P, 3, 2, WCH]), sb("o_p", [P, 2, T])
        sq, total, rstd, gate = sb("o_sq", [P, T]), sb("o_sumsq", [P, T]), sb("o_rstd", [P, T]), sb("o_gate", [P, 2, T])
        mm, pp, tr = ps("o_mm", [P, 2, 2, CH]), ps("o_pp", [P, 2, CH]), ps("o_tr", [P, 2, CH])
        rows = h[:].rearrange("p k t -> p (k t)")[:, 0:4 * D].rearrange("p (s d) -> p s d", s=4)
        cat_in, x_in, p_in = [sem(f"o_cat_in{t}") for t in range(NT)], sem("o_x_in"), sem("o_p_in")
        w_in, proj_in = [sem("o_w_in0"), sem("o_w_in1")], [sem(f"o_proj_in{i}") for i in range(3)]
        tr_done, hi_done, lo_done = sem("o_tr_done"), sem("o_hi_done"), sem("o_lo_done")
        whi_done, wlo_done, mm_done, added = sem("o_whi_done"), sem("o_wlo_done"), sem("o_mm_done"), sem("o_added")
        squared, summed, ssq_done, rstd_ready = sem("o_squared"), sem("o_summed"), sem("o_ssq_done"), sem("o_rstd_ready")
        hhi_done, hlo_done = sem("o_hhi_done"), sem("o_hlo_done")
        scaled, gate_ready, y_ready, stored = sem("o_scaled"), sem("o_gate_ready"), sem("o_y_ready"), sem("o_stored")
        act_step, dve_step = sem("o_act"), sem("o_dve")
        block = ctx.enter_context(nc.Block())
        w_view = [a[name].rearrange("(k p) n -> p k n", p=P) for name in ("w_out", "ple_gate")]
        proj_view = a["ple_proj"].rearrange("(k p) n -> p k n", p=P)
        halved = lambda ap: ap.rearrange("p (x t) -> p x t", x=2)

        @block.sync
        def _(sp):
            def load(c):
                w, n = divmod(c, NC)
                if c >= 2:
                    sp.wait_ge(wlo_done, 2 * c - 2)
                for ks in (slice(0, KD // 2), slice(KD // 2, KD)):
                    sp.dma_start(raw[:, c % 2, ks, :], w_view[w][:, ks, n * WCH:(n + 1) * WCH]).then_inc(w_in[c % 2], 16)
                if w == 1:
                    sp.wait_ge(mm_done, 2 * c - 4)
                    sp.dma_start(proj[:, n % 3], proj_view[:, :, n * WCH:(n + 1) * WCH]).then_inc(proj_in[n % 3], 16)

            def store(j):
                sp.wait_ge(y_ready, j + 1)
                sp.dma_start(o["y_prompt"][j * P:(j + 1) * P, :], h[:, j, 0:TP]).then_inc(stored, 16)
                sp.dma_start(o["y_sample"][j * P:(j + 1) * P, :], h[:, j, TP:T]).then_inc(stored, 16)

            load(0)
            for t, (t0, n) in enumerate(TILES):
                if t == 4:
                    sp.wait_ge(tr_done, GT)
                sp.dma_start(rows[0:n, t % 4, :], B.cat_dram[t0:t0 + n, :]).then_inc(cat_in[t], 16)
            load(1)
            sp.dma_start(pfm[:], a["p_fm"]).then_inc(p_in, 16)
            sp.wait_ge(tr_done, NG)
            sp.dma_start(h[:], a["x_fm"]).then_inc(x_in, 16)
            for c in range(2, 2 * NC):
                load(c)
                if c - NC >= 3:
                    store(2 * (c - NC) - 6)
                    store(2 * (c - NC) - 5)
            for j in range(KD - 6, KD):
                store(j)
            sp.wait_ge(stored, 32 * KD)

        @block.tensor
        def _(pe):
            for t, (t0, n) in enumerate(TILES):
                pe.wait_ge(cat_in[t], 16)
                for q in range(GT):
                    grp = GT * t + q
                    if grp >= 2:
                        pe.wait_ge(lo_done, grp - 1)
                    for j in range(4):
                        k = 4 * q + j
                        last = nc.tensor.transpose(tr[:, grp % 2, j * P:j * P + n], rows[0:n, t % 4, k * P:(k + 1) * P], B.ident[0:n, 0:n])
                    last.then_inc(tr_done, 1)
            pe.wait_ge(lo_done, NG)
            for j in range(2 * KD):
                pe.wait_ge(whi_done, j + 1)
                pe.wait_ge(wlo_done, j + 1)
                if 2 <= j < KD + 2:
                    pe.wait_ge(added, j - 1)
                elif j >= KD + 2:
                    pe.wait_ge(scaled, j - KD - 1)
                if j == KD:
                    pe.wait_ge(summed, KD)
                    for x, cols in enumerate(halves):
                        last = nc.tensor.matmul(tr[:, x, 0:HALF], B.ones[:], total[:, cols], start=True, stop=True)
                    last.then_inc(ssq_done, 1)
                for k in range(KD):
                    if j == KD:
                        pe.wait_ge(hlo_done, k + 1)
                    parts = ((whi, fhi), (whi, flo), (wlo, fhi))
                    for i, (w, f) in enumerate(parts):
                        for x, cols in enumerate(halves):
                            last = nc.tensor.matmul(mm[:, j % 2, x, 0:HALF], w[:, j % 2, k, :], f[:, k, cols],
                                                    start=k == 0 and i == 0, stop=k == KD - 1 and i == 2)
                if j >= KD:
                    jj = j - KD
                    n = jj // 2
                    if jj == 0:
                        pe.wait_ge(p_in, 16)
                    pe.wait_ge(proj_in[n % 3], 16 * (n // 3 + 1))
                    if jj >= 1:
                        pe.wait_ge(y_ready, jj)
                    for k in range(2):
                        for x, cols in enumerate(halves):
                            last = nc.tensor.matmul(pp[:, x, 0:HALF], proj[:, n % 3, k, (jj % 2) * P:(jj % 2 + 1) * P], pfm[:, k, cols],
                                                    start=k == 0, stop=k == 1)
                last.then_inc(mm_done, 1)

        @block.scalar
        def _(act):
            s_ = nc.scalar
            step = Chain(act, act_step)

            def high(j):
                if j >= 2 * KD:
                    return
                c = j // 2
                act.wait_ge(w_in[c % 2], 32 * (c // 2 + 1))
                if j >= 2:
                    act.wait_ge(mm_done, j - 1)
                s_.activation(whi[:, j % 2], raw[:, c % 2, :, (j % 2) * P:(j % 2 + 1) * P], ACT.Copy).then_inc(whi_done, 1)

            high(0)
            for t, (t0, n) in enumerate(TILES):
                for q in range(GT):
                    grp = GT * t + q
                    act.wait_ge(tr_done, grp + 1)
                    s_.activation(fhi[:, 4 * q:4 * q + 4, t0:t0 + n], tr[:, grp % 2, :].rearrange("p (k r) -> p k r", r=P)[:, :, 0:n],
                                  ACT.Copy).then_inc(hi_done, 1)
            high(1)
            for j in range(KD):
                act.wait_ge(added, j + 1)
                if j >= 1:
                    act.wait_ge(summed, j)
                s_.activation(sq[:], h[:, j, :], ACT.Square).then_inc(squared, 1)
                high(j + 2)
            for k in range(KD):
                act.wait_ge(mm_done, KD)
                s_.activation(fhi[:, k, :], h[:, k, :], ACT.Copy, scale=B.plenw[:, k:k + 1]).then_inc(hhi_done, 1)
            act.wait_ge(ssq_done, 1)
            step(s_.activation(halved(rstd[:]), tr[:, :, 0:HALF], ACT.Ln, bias=B.eps[:, 0:1], scale=1.0 / D))
            s_.activation(rstd[:], rstd[:], ACT.Exp, scale=-0.5).then_inc(rstd_ready, 1)
            for j in range(KD):
                act.wait_ge(scaled, j + 1)
                e = gate[:, j % 2, :]
                step(s_.activation(e, e, ACT.Exp, scale=-1.0))
                step(s_.activation(e, e, ACT.Ln, bias=1.0))
                s_.activation(e, e, ACT.Exp, scale=-1.0).then_inc(gate_ready, 1)
                high(KD + j + 2)

        @block.vector
        def _(dve):
            v = nc.vector
            step = Chain(dve, dve_step)

            def low(j):
                if j >= 2 * KD:
                    return
                dve.wait_ge(whi_done, j + 1)
                v.tensor_tensor(wlo[:, j % 2], raw[:, (j // 2) % 2, :, (j % 2) * P:(j % 2 + 1) * P], whi[:, j % 2].bitcast(F32),
                                ALU.subtract).then_inc(wlo_done, 1)

            low(0)
            for t, (t0, n) in enumerate(TILES):
                for q in range(GT):
                    grp = GT * t + q
                    dve.wait_ge(hi_done, grp + 1)
                    v.tensor_tensor(flo[:, 4 * q:4 * q + 4, t0:t0 + n], tr[:, grp % 2, :].rearrange("p (k r) -> p k r", r=P)[:, :, 0:n],
                                    fhi[:, 4 * q:4 * q + 4, t0:t0 + n].bitcast(F32), ALU.subtract).then_inc(lo_done, 1)
            low(1)
            dve.wait_ge(x_in, 16)
            for j in range(KD):
                dve.wait_ge(mm_done, j + 1)
                v.tensor_tensor(halved(h[:, j, :]), halved(h[:, j, :]), mm[:, j % 2, :, 0:HALF], ALU.add).then_inc(added, 1)
                low(j + 2)
            for k in range(KD):
                dve.wait_ge(hhi_done, k + 1)
                v.scalar_tensor_tensor(flo[:, k, :], h[:, k, :], B.plenw[:, k:k + 1], fhi[:, k, :].bitcast(F32),
                                       ALU.mult, ALU.subtract).then_inc(hlo_done, 1)
            dve.wait_ge(rstd_ready, 1)
            for j in range(KD):
                dve.wait_ge(mm_done, KD + j + 1)
                v.tensor_tensor(halved(gate[:, j % 2, :]), mm[:, j % 2, :, 0:HALF], halved(rstd[:]), ALU.mult).then_inc(scaled, 1)
                low(KD + j + 2)
                dve.wait_ge(gate_ready, j + 1)
                step(v.tensor_tensor(halved(gate[:, j % 2, :]), halved(gate[:, j % 2, :]), pp[:, :, 0:HALF], ALU.mult))
                v.tensor_tensor(h[:, j, :], h[:, j, :], gate[:, j % 2, :], ALU.add).then_inc(y_ready, 1)

        @block.gpsimd
        def _(pool):
            for j in range(KD):
                pool.wait_ge(squared, j + 1)
                if j == 0:
                    nc.gpsimd.tensor_copy(total[:], sq[:]).then_inc(summed, 1)
                else:
                    pool.wait_ge(summed, j)
                    nc.gpsimd.tensor_tensor(total[:], total[:], sq[:], ALU.add).then_inc(summed, 1)


def slot_outs(units, slot, outdma, u, nstg):
    return sum(1 for v in outdma if v <= u and slot[v] % nstg == slot[u] % nstg)


def step_kernel(nc, a, o):
    ctx = ExitStack()
    with ctx:
        B = Buffers()
        sb = lambda n, s, d=F32: ctx.enter_context(nc.sbuf_tensor(n, s, d))
        B.ident = sb("ident", [P, P])
        B.ones = sb("ones", [P, P])
        B.eps = sb("eps", [P, 1])
        B.plenw = sb("plenw", [P, KD])
        mixers = ctx.enter_context(ExitStack())
        mix = lambda n, s, d=F32: mixers.enter_context(nc.sbuf_tensor(n, s, d))
        B.fold = mix("fold", [P, 32])
        B.unfold = mix("unfold", [32, P])
        B.newmask = mix("newmask", [P, NB * (TSA + TS)])
        B.winmask = mix("winmask", [P, TS])
        B.normw = mix("normw", [P, KD])
        B.convw = mix("convw", [P, 8, CONV])
        B.convb = mix("convb", [P, 8])
        B.qnw = mix("qnw", [P, 1])
        B.knw = mix("knw", [P, 3 * AD])
        B.cw2 = mix("cw2", [P, AD])
        B.bif = mix("bif", [MH, 2])
        B.m0 = mix("m0_row", [MH, NB])
        B.ptab = mix("ptab", [1, NB * NPG], I32)
        B.wide = mix("wide", [P, NPG * CH])
        B.hbias, B.hbias_neg = mix("hbias", [P, 1]), mix("hbias_neg", [P, 1])
        B.qblk = mix("qblk", [P, 2, NB, 64])
        B.ksel_new = mix("ksel_new", [P, 2, TSA])
        B.kwin_new = mix("kwin_new", [P, 2, TSA])
        B.vsel_new = mix("vsel_new", [TSA, KV * AD])
        B.vwin_new = mix("vwin_new", [TSA, KV * AD])
        B.gsig = mix("gsig", [P, 5, 3 * AH])
        B.comp0_in, B.win_kept = (ctx.enter_context(nc.semaphore(n)) for n in ("comp0_in", "win_kept"))
        B.cat_dram = nc.dram_tensor("cat_scratch", (T, D), F32, kind="Internal").ap()
        B.gates_dram = nc.dram_tensor("gates_scratch", (3, T, MW), F32, kind="Internal").ap()
        B.o_dram = nc.dram_tensor("o_scratch", (3, NB, TS, AW), F32, kind="Internal").ap()

        with ExitStack() as prompt:
            hold = lambda c, n, s, d=F32: c.enter_context(nc.sbuf_tensor(n, s, d))
            B.causal = hold(prompt, "causal", [P, P])
            B.cmpmask = hold(prompt, "cmpmask", [P, 4, 32])
            B.blockdiag = hold(prompt, "blockdiag", [TSA, NB, TS])
            B.member = hold(prompt, "member", [TSA, NB])
            B.headsel = hold(prompt, "headsel", [MH, MH, P])
            B.keep = hold(prompt, "keep", [MH, T])
            B.restart = hold(prompt, "restart", [MH, T])
            B.graw = hold(prompt, "graw", [P, 5, NGATE])
            B.qT = hold(prompt, "qT", [P, 8, TP])
            B.ksel = hold(prompt, "ksel", [P, KV, TP])
            B.kwin = hold(prompt, "kwin", [P, KV, TP])
            B.vsel = hold(prompt, "vsel", [P, 4, KV * AD])
            B.vwin = hold(prompt, "vwin", [P, 4, KV * AD])
            B.cmpin = hold(prompt, "cmpin", [P, 4, CH])
            with ExitStack() as mixer:
                B.upad = hold(mixer, "upad", [P, 8, PADW + NB * SPAD])
                with ExitStack() as x:
                    B.wb = B.wide[:].rearrange("p (x k c) -> p x k c", x=2, k=KD)
                    B.feat = hold(x, "feat", [P, KD, T])
                    constants(nc, B, a)
                    project_in(nc, B, a, o)
                B.cols = hold(mixer, "mcols", [P, 5, 4, MH])
                B.mbc = hold(mixer, "mbc", [P, MH, T])
                B.decbc = hold(mixer, "decbc", [P, MH, NB])
                gate_rows(nc, B, a, o)
                mlstm_heads(nc, B, a, o)
            B.cw1 = hold(prompt, "cw1_prompt", [P, 2, 8, P])
            B.kcT = hold(prompt, "kcT", [P, KV, 32])
            B.vblk = hold(prompt, "vblk", [P, KV, GRP, AD])
            B.comp = B.wide[:].rearrange("p (n c) -> p n c", c=CH)
            compress_prompt(nc, B, a)
            attend_prompt(nc, B, a, o)
        attend_samples(nc, B, a, o)
        combine_samples(nc, B, a, o)
        mixers.close()
        project_out(nc, B, a, o)


def lay_out(i):
    g = lambda n: np.asarray(i[n])
    c = np.ascontiguousarray
    x = np.concatenate([g("x_prompt")[0], g("x_sample").reshape(64, 2048)], 0)
    fm = lambda v: c(v.reshape(-1, 128).T)
    kv = g("cache_nsa_kv")[0]
    npool = kv.shape[0]
    cmp_ = kv[:, :, 0:2].reshape(npool, 8, 8, 2, 2, 4, 64).transpose(0, 3, 6, 2, 4, 1, 5).reshape(npool, 128, 512)
    kt = kv[:, :, 2].reshape(npool, 128, 2, 2, 64).transpose(0, 3, 4, 2, 1).reshape(npool, 128, 256)
    vt = kv[:, :, 3].reshape(npool, 128, 256)
    win = g("cache_win_kv")[0]
    wk = win[:, :, 0].reshape(8, 512, 2, 2, 64).transpose(0, 3, 4, 2, 1).reshape(8, 128, 1024)
    wv = win[:, :, 1].reshape(8, 4, 128, 256).transpose(0, 2, 1, 3).reshape(8, 128, 1024)
    p = np.concatenate([g("p_prompt")[0, 0], g("p_sample")[0].reshape(64, 256)], 0)
    w1 = g("cmp_w1")[0].reshape(2, 2, 8, 2, 64, 64)
    pe = g("cmp_pe")[0].reshape(2, 2, 8, 2, 64)
    return {
        "x_fm": c(x.T.reshape(16, 128, 576).transpose(1, 0, 2)),
        "norm_w": fm(g("norm_w")[0]), "ple_norm": fm(g("ple_norm")[0]),
        "w_in": g("w_in")[0], "w_out": g("w_out")[0], "ple_gate": g("ple_gate")[0], "ple_proj": g("ple_proj")[0],
        "conv_w": c(g("m_conv_w")[0].reshape(4, 8, 128).transpose(2, 1, 0)), "conv_b": fm(g("m_conv_b")[0]),
        "conv_state": c(g("state_mlstm_conv")[0].reshape(8, 3, 8, 128).transpose(3, 2, 0, 1)),
        "wq": g("m_wq")[0], "wk": g("m_wk")[0], "wv": g("m_wv")[0],
        "b_if": c(np.stack([g("m_b_i")[0], g("m_b_f")[0]], 1)), "m0": c(g("state_mlstm_m")[0].T),
        "m_norm_w": g("m_norm_w")[0].reshape(1024),
        "a_q_norm": g("a_q_norm")[0], "a_k_norm": g("a_k_norm")[0],
        "pages": c(np.concatenate([cmp_, kt, vt], 2)), "page_table": c(g("page_table").reshape(1, 256)),
        "win_pages": c(np.concatenate([wk, wv], 2)), "win_rows": c(win.reshape(8, 512, 512)),
        "state": c(np.concatenate([g("state_mlstm_C")[0], g("state_mlstm_n")[0][..., None]], 3)),
        "cmp_w1": c(w1.transpose(3, 4, 0, 2, 1, 5).reshape(128, 2, 8, 128)),
        "cmp_w2": g("cmp_w2")[0].reshape(128, 64), "cmp_pe": c(pe.transpose(3, 4, 0, 1, 2).reshape(128, 2, 2, 8)),
        "p_fm": c(p.T.reshape(2, 128, 576).transpose(1, 0, 2)),
    }


OUTS = {
 "y_prompt": ((2048, 512), (1, 512, 2048)), "y_sample": ((2048, 64), (8, 8, 2048)),
 "kv_prompt": ((512, 1024), (1, 1, 512, 4, 4, 64)), "kv_sample": ((64, 1024), (1, 8, 8, 4, 4, 64)),
 "win_prompt": ((512, 512), (1, 1, 512, 2, 4, 64)), "win_sample": ((8, 512, 512), (1, 8, 512, 2, 4, 64)),
 "C_prompt": ((4, 256, 256), (1, 1, 4, 256, 256)), "n_prompt": ((4, 256), (1, 1, 4, 256)), "m_prompt": ((4, 1), (1, 1, 4)),
 "conv_prompt": ((3, 1024), (1, 1, 3, 1024)),
 "C_sample": ((8, 4, 256, 256), (1, 8, 4, 256, 256)), "n_sample": ((8, 4, 256), (1, 8, 4, 256)), "m_sample": ((4, 8), (1, 8, 4)),
 "conv_sample": ((8, 3, 1024), (1, 8, 3, 1024)),
}


def kernel(**inputs):
    import concourse.bacc as bacc
    from concourse.bass_utils import run_bass_kernel_spmd

    nc = bacc.Bacc("TRN2", target_bir_lowering=False, num_devices=1)
    arrays = {name: np.ascontiguousarray(v) for name, v in lay_out(inputs).items()}
    ins = {name: nc.dram_tensor(name, v.shape, mybir.dt.from_np(v.dtype), kind="ExternalInput").ap()
           for name, v in arrays.items()}
    outs = {name: nc.dram_tensor(name, shape, F32, kind="ExternalOutput").ap() for name, (shape, _) in OUTS.items()}
    step_kernel(nc, ins, outs)
    result = run_bass_kernel_spmd(nc, [arrays], core_ids=[0]).results[0]
    turned = lambda name: result[name].T if name in ("y_prompt", "y_sample", "m_sample") else result[name]
    return tuple(turned(name).reshape(shape) for name, (_, shape) in OUTS.items())
```
